# Optimizing a Trainium2 kernel written in Bass

```python
import jax, jax.numpy as jnp
from jax import lax
import numpy as np

D_MODEL = 1024
BATCH = 1
SEQ = 512
DEPTH = 2
DEC_BATCH = 8
DEC_SEQ = 8
PAST_LEN = 256
PAGE_SIZE = 128

N_A = DEPTH // 2
N_B = DEPTH - N_A
CONV_W = 31
N_HEADS = 16
N_KV = 4
GROUP = N_HEADS // N_KV
HEAD_DIM = D_MODEL // N_HEADS
KV_W = N_KV * HEAD_DIM
Q_W = N_HEADS * HEAD_DIM
L_CMP = 32
STRIDE = 16
CMP_R = L_CMP // STRIDE
CMP_HID = 2 * HEAD_DIM
L_SEL = 64
TOP_N = 16
WINDOW = 512
Q_BLK = 128
D_FF = (8 * D_MODEL + 3 * 256 - 1) // (3 * 256) * 256
N_MOD = 6 * DEPTH + 4
EPS = 1e-6
FORCE = 1e3
NEG = -1e30

kernel_name = 'yoco_conformer_nsa_decoder_step'

def rmsnorm(x, g):
    xf = x.astype(jnp.float32)
    y = xf * lax.rsqrt(jnp.mean(xf * xf, axis=-1, keepdims=True) + EPS)
    return (y * g.astype(jnp.float32)).astype(x.dtype)

def modulate(x, g, shift, scale):
    return rmsnorm(x, g) * (1 + scale[:, None, :]) + shift[:, None, :]

def layernorm(x, g, b):
    xf = x.astype(jnp.float32)
    mu = jnp.mean(xf, axis=-1, keepdims=True)
    var = jnp.mean(jnp.square(xf - mu), axis=-1, keepdims=True)
    y = (xf - mu) * lax.rsqrt(var + EPS) * g.astype(jnp.float32) + b.astype(jnp.float32)
    return y.astype(x.dtype)

def alibi_slopes():
    return jnp.exp2(-8.0 * jnp.arange(1, N_HEADS + 1, dtype=jnp.float32) / N_HEADS)

def masked_softmax(s, mask):
    p = jax.nn.softmax(jnp.where(mask, s, NEG), axis=-1)
    return jnp.where(mask, p, 0.0)

def swiglu(h, w_up, w_down):
    a = h @ w_up
    return (jax.nn.silu(a[..., :D_FF]) * a[..., D_FF:]) @ w_down

def conv_module(h, prev, w_pw1, b_pw1, w_dw, b_dw, ln_g, ln_b, w_pw2):
    a = h @ w_pw1 + b_pw1
    u = a[..., :D_MODEL] * jax.nn.sigmoid(a[..., D_MODEL:])
    up = jnp.concatenate([prev.astype(u.dtype), u], axis=1)
    y = lax.conv_general_dilated(up, w_dw[:, None, :].astype(up.dtype), (1,), 'VALID',
                                 dimension_numbers=('NWC', 'WIO', 'NWC'),
                                 feature_group_count=D_MODEL) + b_dw
    y = jax.nn.silu(layernorm(y, ln_g, ln_b))
    return y @ w_pw2, up[:, -(CONV_W - 1):]

def compress(x, w1, w2, pe):
    B, T = x.shape[0], x.shape[1]
    n_c = (T - L_CMP) // STRIDE + 1
    n_half = -(-T // STRIDE)
    xp = jnp.pad(x, ((0, 0), (0, n_half * STRIDE - T), (0, 0), (0, 0)))
    xp = xp.reshape(B, n_half, STRIDE, N_KV, HEAD_DIM)
    parts = []
    for r in range(CMP_R):
        seg = slice(r * STRIDE, (r + 1) * STRIDE)
        pr = jnp.einsum('bnlkd,lde->bnke', xp, w1[seg]) + jnp.einsum('ld,lde->e', pe[seg], w1[seg])
        parts.append(pr[:, r:r + n_c])
    hid = sum(parts[1:], parts[0])
    return jnp.einsum('bnke,ed->bnkd', jax.nn.silu(hid), w2)

def sel_blocks(x):
    B, T = x.shape[0], x.shape[1]
    n_s = -(-T // L_SEL)
    xp = jnp.pad(x, ((0, 0), (0, n_s * L_SEL - T), (0, 0), (0, 0)))
    return xp.reshape(B, n_s, L_SEL, N_KV, HEAD_DIM).transpose(0, 3, 1, 2, 4)

def build_ctx(kv4, w_cmp1, w_cmp2, pe_cmp):
    kc = compress(kv4[:, :, 0], w_cmp1[0], w_cmp2[0], pe_cmp[0])
    vc = compress(kv4[:, :, 1], w_cmp1[1], w_cmp2[1], pe_cmp[1])
    ksb = sel_blocks(kv4[:, :, 2])
    vsb = sel_blocks(kv4[:, :, 3])
    n_c, n_s = kc.shape[1], ksb.shape[2]
    cend = jnp.arange(n_c, dtype=jnp.int32) * STRIDE + (L_CMP - 1)
    i0 = jnp.arange(n_c)[:, None] * STRIDE
    j0 = jnp.arange(n_s)[None, :] * L_SEL
    m_sel = ((i0 < j0 + L_SEL) & (i0 + L_CMP > j0)).astype(jnp.float32)
    return (kc, vc, cend, m_sel, ksb, vsb)

def nsa_core(q, gate, qpos, ctx, kw, vw, kwpos, slopes):
    kc, vc, cend, m_sel, ksb, vsb = ctx
    B, Q = q.shape[0], q.shape[1]
    scale = HEAD_DIM ** -0.5
    sl = slopes.reshape(1, 1, N_KV, GROUP, 1)
    d_c = (qpos[:, None] - cend[None, :]).astype(jnp.float32)[None, :, None, None, :]
    s_c = jnp.einsum('bqkgd,bnkd->bqkgn', q, kc).astype(jnp.float32) * scale - sl * d_c
    p_c = masked_softmax(s_c, d_c >= 0)
    o_c = jnp.einsum('bqkgn,bnkd->bqkgd', p_c.astype(vc.dtype), vc)
    n_s = m_sel.shape[1]
    imp = jnp.einsum('bqkgn,ns->bqks', p_c, m_sel)
    blk = jnp.arange(n_s, dtype=jnp.int32)[None, :]
    cur = (qpos // L_SEL)[:, None]
    valid = (blk * L_SEL <= qpos[:, None])[None, :, None, :]
    forced = ((blk == 0) | (blk == cur) | (blk == cur - 1))[None, :, None, :]
    score = jnp.where(valid, imp + jnp.where(forced, FORCE, 0.0), -jnp.inf)
    _, idx = lax.top_k(score, min(TOP_N, n_s))
    bi = jnp.arange(B)[:, None, None, None]
    ki = jnp.arange(N_KV)[None, None, :, None]
    ks = ksb[bi, ki, idx]
    vs = vsb[bi, ki, idx]
    pos = idx[..., None] * L_SEL + jnp.arange(L_SEL, dtype=jnp.int32)
    d_s = (qpos[None, :, None, None, None] - pos).astype(jnp.float32)[:, :, :, None]
    s_s = jnp.einsum('bqkgd,bqknld->bqkgnl', q, ks).astype(jnp.float32) * scale - sl[..., None] * d_s
    shp = s_s.shape
    p_s = masked_softmax(s_s.reshape(shp[:4] + (-1,)), (d_s >= 0).reshape(B, Q, N_KV, 1, -1)).reshape(shp)
    o_s = jnp.einsum('bqkgnl,bqknld->bqkgd', p_s.astype(vs.dtype), vs)
    d_w = qpos[:, None] - kwpos[None, :]
    m_w = ((d_w >= 0) & (d_w < WINDOW) & (kwpos >= 0)[None, :])[None, :, None, None, :]
    s_w = jnp.einsum('bqkgd,btkd->bqkgt', q, kw).astype(jnp.float32) * scale \
        - sl * d_w.astype(jnp.float32)[None, :, None, None, :]
    p_w = masked_softmax(s_w, m_w)
    o_w = jnp.einsum('bqkgt,btkd->bqkgd', p_w.astype(vw.dtype), vw)
    g = jax.nn.sigmoid(gate.astype(jnp.float32))
    o = g[..., 0:1] * o_c + g[..., 1:2] * o_s + g[..., 2:3] * o_w
    return o.reshape(B, Q, Q_W).astype(q.dtype)

def nsa_mixer(h, w_in, w_o, ctx, q_blk, pos0, window_fn, slopes):
    B, T = h.shape[0], h.shape[1]
    nb = T // q_blk
    a = h @ w_in
    q = a[..., :Q_W].reshape(B, nb, q_blk, N_KV, GROUP, HEAD_DIM).swapaxes(0, 1)
    g = a[..., Q_W:].reshape(B, nb, q_blk, N_KV, GROUP, 3).swapaxes(0, 1)
    s0 = pos0 + q_blk * jnp.arange(nb, dtype=jnp.int32)

    def one_block(args):
        qi, gi, si = args
        qpos = si + jnp.arange(q_blk, dtype=jnp.int32)
        kw, vw, kwpos = window_fn(si)
        return nsa_core(qi, gi, qpos, ctx, kw, vw, kwpos, slopes)

    o = lax.map(one_block, (q, g, s0))
    return o.swapaxes(0, 1).reshape(B, T, Q_W) @ w_o

def setup_inputs(seed: int = 0) -> dict:
    key = jax.random.key(seed)
    ks = jax.random.split(key, 28)

    def nrm(k, shape, s):
        return jax.random.normal(k, shape, jnp.float32) * s

    n_pages = PAST_LEN // PAGE_SIZE
    n_used = DEC_BATCH * n_pages
    n_pool = n_used + n_used // 4
    page_table = jax.random.permutation(ks[3], n_pool)[:n_used].reshape(DEC_BATCH, n_pages).astype(jnp.int32)
    return {
        'x_prompt': nrm(ks[0], (BATCH, SEQ, D_MODEL), 1.0),
        'x_sample': nrm(ks[1], (DEC_BATCH, DEC_SEQ, D_MODEL), 1.0),
        'cache_kv': nrm(ks[2], (n_pool, PAGE_SIZE, 4, N_KV, HEAD_DIM), 1.0),
        'page_table': page_table,
        'state_win': nrm(ks[4], (DEC_BATCH, min(WINDOW, PAST_LEN), 2, N_KV, HEAD_DIM), 1.0),
        'state_conv': nrm(ks[5], (N_A, DEC_BATCH, CONV_W - 1, D_MODEL), 0.5),
        'c_prompt': nrm(ks[6], (BATCH, D_MODEL), 1.0),
        'c_sample': nrm(ks[7], (DEC_BATCH, D_MODEL), 1.0),
        'w_ada': nrm(ks[8], (D_MODEL, N_MOD * D_MODEL), 0.5 * D_MODEL ** -0.5),
        'b_ada': nrm(ks[9], (N_MOD * D_MODEL,), 0.01),
        'norm_g': 1.0 + nrm(ks[10], (DEPTH, 2, D_MODEL), 0.02),
        'conv_w_pw1': nrm(ks[11], (N_A, D_MODEL, 2 * D_MODEL), D_MODEL ** -0.5),
        'conv_b_pw1': nrm(ks[12], (N_A, 2 * D_MODEL), 0.01),
        'conv_w_dw': nrm(ks[13], (N_A, CONV_W, D_MODEL), CONV_W ** -0.5),
        'conv_b_dw': nrm(ks[14], (N_A, D_MODEL), 0.01),
        'conv_ln_g': 1.0 + nrm(ks[15], (N_A, D_MODEL), 0.02),
        'conv_ln_b': nrm(ks[16], (N_A, D_MODEL), 0.01),
        'conv_w_pw2': nrm(ks[17], (N_A, D_MODEL, D_MODEL), D_MODEL ** -0.5),
        'ffn_w_up': nrm(ks[18], (DEPTH, D_MODEL, 2 * D_FF), D_MODEL ** -0.5),
        'ffn_w_down': nrm(ks[19], (DEPTH, D_FF, D_MODEL), D_FF ** -0.5),
        'kv_norm_g': 1.0 + nrm(ks[20], (D_MODEL,), 0.02),
        'w_kv': nrm(ks[21], (D_MODEL, 6 * KV_W), D_MODEL ** -0.5),
        'w_cmp1': nrm(ks[22], (2, L_CMP, HEAD_DIM, CMP_HID), (L_CMP * HEAD_DIM) ** -0.5),
        'w_cmp2': nrm(ks[23], (2, CMP_HID, HEAD_DIM), CMP_HID ** -0.5),
        'pe_cmp': nrm(ks[24], (2, L_CMP, HEAD_DIM), 0.1),
        'nsa_w_in': nrm(ks[25], (N_B, D_MODEL, Q_W + 3 * N_HEADS), D_MODEL ** -0.5),
        'nsa_w_o': nrm(ks[26], (N_B, Q_W, D_MODEL), Q_W ** -0.5),
        'final_norm_g': 1.0 + nrm(ks[27], (D_MODEL,), 0.02),
    }

def reference(x_prompt, x_sample, cache_kv, page_table, state_win, state_conv,
              c_prompt, c_sample, w_ada, b_ada, norm_g,
              conv_w_pw1, conv_b_pw1, conv_w_dw, conv_b_dw, conv_ln_g, conv_ln_b, conv_w_pw2,
              ffn_w_up, ffn_w_down, kv_norm_g, w_kv, w_cmp1, w_cmp2, pe_cmp,
              nsa_w_in, nsa_w_o, final_norm_g):
    slopes = alibi_slopes()

    def trunk(x, c, conv_prev, attn_setup):
        B, T = x.shape[0], x.shape[1]
        mods = (jax.nn.silu(c) @ w_ada + b_ada).reshape(B, N_MOD, D_MODEL)
        conv_new = []
        attn, extra = None, None
        for l in range(DEPTH):
            m = mods[:, 6 * l:6 * l + 6]
            if l == N_A:
                k0 = 6 * DEPTH
                hk = modulate(x, kv_norm_g, mods[:, k0], mods[:, k0 + 1])
                kv_new = (hk @ w_kv).reshape(B, T, 6, N_KV, HEAD_DIM)
                attn, extra = attn_setup(kv_new)
            h = modulate(x, norm_g[l, 0], m[:, 0], m[:, 1])
            if l < N_A:
                y, st = conv_module(h, conv_prev[l], conv_w_pw1[l], conv_b_pw1[l], conv_w_dw[l],
                                    conv_b_dw[l], conv_ln_g[l], conv_ln_b[l], conv_w_pw2[l])
                conv_new.append(st)
            else:
                y = attn(h, nsa_w_in[l - N_A], nsa_w_o[l - N_A])
            x = x + m[:, 2][:, None, :] * y
            h = modulate(x, norm_g[l, 1], m[:, 3], m[:, 4])
            x = x + m[:, 5][:, None, :] * swiglu(h, ffn_w_up[l], ffn_w_down[l])
        k0 = 6 * DEPTH + 2
        y = modulate(x, final_norm_g, mods[:, k0], mods[:, k0 + 1])
        return y, extra, jnp.stack(conv_new)

    def prompt_setup(kv_new):
        B, T = kv_new.shape[0], kv_new.shape[1]
        ctx = build_ctx(kv_new[:, :, :4], w_cmp1, w_cmp2, pe_cmp)
        pad = ((0, 0), (WINDOW, 0), (0, 0), (0, 0))
        kw_pad = jnp.pad(kv_new[:, :, 4], pad)
        vw_pad = jnp.pad(kv_new[:, :, 5], pad)

        def window_fn(s0):
            kwpos = s0 - WINDOW + jnp.arange(WINDOW + Q_BLK, dtype=jnp.int32)
            return (lax.dynamic_slice_in_dim(kw_pad, s0, WINDOW + Q_BLK, axis=1),
                    lax.dynamic_slice_in_dim(vw_pad, s0, WINDOW + Q_BLK, axis=1), kwpos)

        def attn(h, w_in, w_o):
            return nsa_mixer(h, w_in, w_o, ctx, Q_BLK, 0, window_fn, slopes)

        kv_pages = kv_new[:, :, :4].reshape(B * T // PAGE_SIZE, PAGE_SIZE, 4, N_KV, HEAD_DIM)
        win = kv_new[:, T - min(WINDOW, T):, 4:6]
        return attn, (kv_pages, win)

    def sample_setup(kv_new):
        Bd, Tn = kv_new.shape[0], kv_new.shape[1]
        past = cache_kv[page_table].reshape(Bd, -1, 4, N_KV, HEAD_DIM)
        full = jnp.concatenate([past, kv_new[:, :, :4].astype(past.dtype)], axis=1)
        ctx = build_ctx(full, w_cmp1, w_cmp2, pe_cmp)
        win_all = jnp.concatenate([state_win, kv_new[:, :, 4:6].astype(state_win.dtype)], axis=1)
        n_buf = state_win.shape[1]
        kwpos = PAST_LEN - n_buf + jnp.arange(n_buf + Tn, dtype=jnp.int32)

        def window_fn(s0):
            return win_all[:, :, 0], win_all[:, :, 1], kwpos

        def attn(h, w_in, w_o):
            return nsa_mixer(h, w_in, w_o, ctx, 1, PAST_LEN, window_fn, slopes)

        n_keep = min(WINDOW, PAST_LEN + Tn)
        return attn, (kv_new[:, :, :4], win_all[:, win_all.shape[1] - n_keep:])

    conv0 = jnp.zeros((N_A, x_prompt.shape[0], CONV_W - 1, D_MODEL), x_prompt.dtype)
    y_prompt, (kv_prompt, win_prompt), conv_prompt = trunk(x_prompt, c_prompt, conv0, prompt_setup)
    y_sample, (kv_sample, win_sample), conv_sample = trunk(x_sample, c_sample, state_conv, sample_setup)
    return (y_prompt, y_sample, kv_prompt, kv_sample, win_prompt, win_sample, conv_prompt, conv_sample)


_drawn_inputs = setup_inputs


def setup_inputs(seed=0):
    import zlib

    import numpy as np

    out = dict(_drawn_inputs(seed))
    spreads = {}
    factors = {'b_ada': 3.013,
     'norm_g': 2.766,
     'conv_b_pw1': 5.7,
     'conv_b_dw': 8.0,
     'conv_ln_g': 8.0,
     'conv_ln_b': 29.374,
     'kv_norm_g': 8.782,
     'pe_cmp': 5.512,
     'final_norm_g': 9.92}
    for name, (base, spread) in spreads.items():
        noise = np.random.default_rng([zlib.crc32(name.encode()), seed]).standard_normal(out[name].shape)
        drawn = base * np.exp(spread * noise) if base else spread * noise
        out[name] = __import__('jax').numpy.asarray(drawn.astype(out[name].dtype))
    for name, factor in factors.items():
        out[name] = (out[name] * factor).astype(out[name].dtype)
    return out
```

```python
from contextlib import ExitStack

import concourse.bass as bass
from concourse import mybir

F32 = mybir.dt.float32
F32R = mybir.dt.float32r
I32 = mybir.dt.int32
ACT = mybir.ActivationFunctionType
ALU = mybir.AluOpType
AX = mybir.AxisListType

P = 128
D = 1024
DC = D // P
TP = 512
NB, NT = 8, 8
TS = NB * NT
T = TP + TS
HT = T // 2
CW = 31
FF = 2816
FH = FF // 2
FHC = FH // P
NH, NKV, G, HD = 16, 4, 4, 64
LC, ST = 32, 16
NCP = (TP - LC) // ST + 1
PAST = 256
NCS = (PAST + NT - LC) // ST + 1
PG = 128
NPG = PAST // PG
EPS = 1e-6
SCALE = HD ** -0.5
NKS = PAST + TS
FAR = 1e32
SLOPES = [2.0 ** (-8.0 * (h + 1) / NH) for h in range(NH)]

R_NG, R_B1, R_BDW, R_LNG, R_LNB, R_KVG, R_FING, R_PE, R_END = 0, 32, 48, 56, 64, 72, 80, 88, 120

NORMS = [(R_NG, 0, 1), (R_NG + 8, 3, 4), (R_KVG, 12, 13), (R_NG + 16, 6, 7), (R_NG + 24, 9, 10), (R_FING, 14, 15)]
STAT_OF = [0, 1, 2, 2, 3, 4]
GATES = [2, 5, 5, 8, 11, 11]

UNITS = []
for _j in range(DC):
    UNITS += [("pw1", 0, DC, _j * P, P), ("pw1", 0, DC, D + _j * P, P)]
U_PW2 = len(UNITS)
UNITS += [("pw2", 0, DC, _m * P, P) for _m in range(DC)]


def _ffn_units(layer):
    out = []
    for hf in range(2):
        for p in range(FHC):
            out += [(f"up{layer}", 0, DC, hf * FH + p * P, P), (f"up{layer}", 0, DC, FF + hf * FH + p * P, P)]
        out += [(f"down{layer}", hf * FH, FHC, m * P, P) for m in range(DC)]
    return out


U_FFN = [len(UNITS), 0]
UNITS += _ffn_units(0)
U_KV = len(UNITS)
UNITS += [("kv", 0, DC, _m * P, P) for _m in range(12)]
U_IN = len(UNITS)
UNITS += [("in", 0, DC, _m * P, P) for _m in range(DC)] + [("in", 0, DC, D, 3 * NH)]
U_WO = len(UNITS)
UNITS += [("wo", 0, DC, _m * P, P) for _m in range(DC)]
U_FFN[1] = len(UNITS)
UNITS += _ffn_units(1)
NU = len(UNITS)
F_UNITS = 2 * FHC + DC
RING = 3
LOOP_PAIRS = 3
LOOPS = FHC // LOOP_PAIRS
assert 2 * LOOP_PAIRS % RING == 0

ADA_COLS = 256
N_ADA = 16 * D // ADA_COLS
ADA_FIRST = 8
ADA_PW1 = 2
ADA_TAIL = N_ADA - ADA_FIRST - ADA_PW1 * U_PW2

KV_SLOT = {4: 0, 5: 1, 8: 2, 9: 3, 0: 4, 1: 5, 2: 6, 3: 7, 6: 8, 7: 9, 10: 10, 11: 11}


def build(nc, a, o, c):
    ctx = ExitStack()
    with ctx:
        sems = {}

        def S(name):
            if name not in sems:
                sems[name] = ctx.enter_context(nc.semaphore(name))
            return sems[name]

        base = [(nc.sbuf_base + 31) // 32 * 32]

        def at(name, shape, off, dt=F32):
            return nc.alloc_sbuf_tensor_at(name, shape, dt, offset=off)

        def place(name, shape, dt=F32):
            n = 4
            for s in shape[1:]:
                n *= s
            off = base[0]
            base[0] += (n + 31) // 32 * 32
            return at(name, shape, off, dt)

        def region(nbytes):
            off = base[0]
            base[0] += (nbytes + 31) // 32 * 32
            return off

        x = place("x", [P, DC, T])
        rH = region(2 * DC * T * 4)
        Hh = at("Hh", [P, DC, T], rH, F32R)
        Hl = at("Hl", [P, DC, T], rH + DC * T * 4, F32R)
        sqb = at("sqb", [P, DC, T], rH)
        xf = at("xf", [P, DC, T], rH)
        rF = region(2 * FHC * T * 4)
        ah = at("ah", [P, FHC, T], rF, F32R)
        al = at("al", [P, FHC, T], rF + FHC * T * 4, F32R)
        u_p = at("u_p", [P, DC, CW - 1 + TP], rF)
        u_s = at("u_s", [P, DC, CW - 1 + NT, NB], rF + DC * (CW - 1 + TP) * 4)
        y = at("y", [P, DC, T], rF + (DC * (CW - 1 + TP) + DC * NB * (CW - 1 + NT)) * 4)
        assert DC * (CW - 1 + TP) + DC * NB * (CW - 1 + NT) + DC * T <= 2 * FHC * T
        rows0 = at("rows0", [P, 5, P], rF + DC * (CW - 1 + TP) * 4 + DC * NB * (CW - 1 + NT) * 4)
        kvT = at("kvT", [P, 12, T], rF)
        oT = at("oT", [P, DC, T], rF + 4 * T * 4)
        qT = at("qT", [P, DC, T], rF + 12 * T * 4)
        off = rF + 20 * T * 4
        kcT_p = at("kcT_p", [P, 2, NCP], off)
        vc_p = at("vc_p", [32, NKV, HD], off + 256)
        kcT_s = at("kcT_s", [P, 2, NB, NCS], off + 1280)
        hv_s = at("hv_s", [P, NB * NKV * NCS], off + 2240)
        assert off + 2240 + 1920 <= rF + 2 * FHC * T * 4
        raw = place("raw", [P, RING, FHC, P])
        wh = place("wh", [P, RING, FHC, P], F32R)
        wl = place("wl", [P, RING, FHC, P], F32R)
        mods = place("mods", [P, 16 * DC, 1 + NB])
        rA = region(3 * DC * ADA_COLS * 4)
        ada = at("ada", [P, 3, DC, ADA_COLS], rA)
        vrow = at("vrow", [P, 5, 2, NKV, HD], rA)
        o1 = rA + 5 * 512 * 4
        bias = at("bias", [P, G, TP], o1)
        winst = at("winst", [P, 2, 512], o1)
        w1k = at("w1k", [P, LC // 2, P], o1)
        vc_s = at("vc_s", [NCS, NB, NKV, HD], o1)
        o2 = o1 + 8192
        PT = at("PT", [P, 2, G * P], o2)
        PTs = at("PTs", [P, 7, P], o2)
        expd = at("expd", [3 * NH, 3, P], o2)
        Cb = [None, at("C1", [P, 2 * NKV, 2, HD], o2)]
        o3 = o2 + 4096
        gates = at("gates", [P, 4, NH, 3], o3)
        gs = at("gs", [P, 3, NB], o3 + 768)
        nmin = at("nmin", [P, 2, 12], o3 + 896)
        sums = at("sums", [P, 2, 12], o3 + 1024)
        wgt = at("wgt", [P, 2, 12], o3 + 1152)
        peb = at("peb", [P, 2], o3 + 1280)
        assert o3 + 1312 <= rA + 3 * DC * ADA_COLS * 4
        CPk = at("CPk", [P, 4, NKV, P], rH)
        CPv = at("CPv", [P, 4, NKV, P], rH + 8192)
        P2 = at("P2", [P, 2 * NKV, TP // 2], rH + 16384)
        w1v = at("w1v", [P, LC // 2, P], rH + 24576)
        Cb[0] = at("C0", [P, 2 * NKV, 2, HD], rH + 32768)
        Pp = at("Pp", [P, 2, 8, TP], rH)
        Pc = at("Pc", [P, 2, G, NCP], rH + 32768)
        tabs = at("tabs", [P, NB, NKS], rH)
        Ps = at("Ps", [P, 2, 2, NKS], rH + 10240)
        Pcs = at("Pcs", [P, 2, 16], rH + 15360)
        Cs = at("Cs", [P, 2, 2, 512], rH + 15488)
        Cw = at("Cw", [P, 2, 2, 512], rH + 15488 + 8192)
        KT = at("KT", [P, 2, 2, 2, P], rH + 15488 + 16384)
        assert 15488 + 16384 + 4096 <= 2 * DC * T * 4
        t2 = place("t2", [P, 2, T])
        r = place("r", [P, T])
        rMu = region(T * 4)
        mu = at("mu", [P, T], rMu)
        dist = at("dist", [P, TP], rMu)
        rS = region(DC * TS * 4)
        fs = at("fs", [P, DC, TS], rS)
        qs = at("qs", [P, 2, NB, G, NT], rS)
        stage = place("stage", [P, 2, D])
        ident = place("ident", [P, P])
        ones = place("ones", [P, P])
        vT = place("vT", [P, R_END])
        wdT = place("wdT", [P, CW * DC])
        rB = region(P * 4)
        badaT = at("badaT", [P, P], rB)
        w2t = at("w2t", [P, 2, HD], rB)
        cT = place("cT", [P, 9 * DC])
        acoef = place("acoef", [P, DC, 1 + NB])
        epst = place("epst", [P, 1])
        distc = place("distc", [P, 4, NCP])
        maskc = place("maskc", [P, NCP])
        tmask = place("tmask", [P, NT])
        tabc = place("tabc", [P, NCS])
        rtmp = place("rtmp", [P, 2, TS])
        pgt = place("pgt", [1, NB * NPG], I32)
        assert base[0] <= nc.sbuf_usable_end, (base[0], nc.sbuf_usable_end)

        ps = ctx.enter_context(nc.psum_tensor("ps", [P, 8, 512], F32))

        def tile(u, w=P):
            s = 2 * (u % RING)
            return ps[0:w, s:s + 2, 0:HT]

        def halves(ap):
            return ap.rearrange("p (b t) -> p b t", b=2)

        def smp_cols(t_):
            return t_[:, 1, HT - TS:HT].rearrange("p (b t) -> p b t", b=NB)

        stats = ps[:, 6:8, 0:HT]

        raw_in = [S(f"raw_in{i}") for i in range(RING)]
        hi_ready, lo_ready = S("hi_ready"), S("lo_ready")
        tile_done, tile_free = S("tile_done"), S("tile_free")
        ada_in = [S(f"ada_in{i}") for i in range(3)]
        ada_used, ada_ev = S("ada_used"), S("ada_ev")
        x_upd = S("x_upd")

        W = {"pw1": a["conv_w_pw1"][0], "pw2": a["conv_w_pw2"][0], "kv": a["w_kv"],
             "in": a["nsa_w_in"][0], "wo": a["nsa_w_o"][0],
             "up0": a["ffn_w_up"][0], "up1": a["ffn_w_up"][1],
             "down0": a["ffn_w_down"][0], "down1": a["ffn_w_down"][1]}
        wada = a["w_ada"].rearrange("(c p) n -> p c n", p=P)

        def load_unit(sp, u, slot=None, shift=0, turn=None):
            name, r0, K, c0, w = UNITS[u]
            slot = u % RING
            src = W[name][r0:r0 + K * P, :].rearrange("(c p) n -> p c n", p=P)
            sp.dma_start(raw[:, slot, 0:K, 0:w], src[:, :, bass.ds(c0 + shift, w)]).then_inc(raw_in[slot], 16)

        def load_ada(sp, n):
            if n >= 3:
                sp.wait_ge(ada_used, n - 2)
            sp.dma_start(ada[:, n % 3], wada[:, :, n * ADA_COLS:(n + 1) * ADA_COLS]).then_inc(ada_in[n % 3], 16)

        SPLIT_AHEAD = 2
        xi_rows = [P, P, P, P, TS, 120, 120]
        page_rows = a["cache_kv"].rearrange("n (q e) t h d -> n q e (t h d)", e=2)
        win_rows = a["state_win"].rearrange("b (q e) t h d -> b q e (t h d)", e=2)
        kvp = o["kv_prompt"].rearrange("n s t h d -> n s (t h d)")
        kvs = o["kv_sample"].rearrange("b s t h d -> (b s) (t h d)")
        wps = o["win_prompt"].rearrange("b (n s) t h d -> (b n) s (t h d)", s=P)
        wss = o["win_sample"].rearrange("b s t h d -> b s (t h d)")

        pt0 = [0]
        for n in range(4 * NKV):
            pt0.append(pt0[-1] + 2 * (n % 4 + 1) + 1)

        block = ctx.enter_context(nc.Block())

        @block.sync
        def _(sp):
            sp.dma_start(ident[:], c["ident"]).then_inc(S("id_in"), 16)
            vrows = rows0[0:R_END, 0, :]
            at_row = 0
            for name, n in (("norm_g", 32), ("conv_b_pw1", 16), ("conv_b_dw", 8), ("conv_ln_g", 8),
                            ("conv_ln_b", 8), ("kv_norm_g", 8), ("final_norm_g", 8), ("pe_cmp", 32)):
                flat = a[name]
                dims = "abcd"[:len(flat.shape)]
                if len(dims) > 1:
                    flat = flat.rearrange(f"{' '.join(dims)} -> ({' '.join(dims)})")
                sp.dma_start(vrows[at_row:at_row + n, :], flat.rearrange("(r p) -> r p", p=P)).then_inc(S("vec_in"), 16)
                at_row += n
            wd = a["conv_w_dw"].rearrange("a w (c p) -> (a w c) p", p=P)
            for i in range(2):
                sp.dma_start(rows0[0:124, 1 + i, :], wd[124 * i:124 * i + 124, :]).then_inc(S("vec_in"), 16)
            sp.dma_start(rows0[:, 3, :], a["b_ada"].rearrange("(r p) -> r p", p=P)).then_inc(S("vec_in"), 16)
            sp.dma_start(rows0[0:8, 4, :], a["c_prompt"].rearrange("b (k p) -> (b k) p", p=P)).then_inc(S("c_in"), 16)
            sp.dma_start(rows0[8:72, 4, :], a["c_sample"].rearrange("b (k p) -> (b k) p", p=P)).then_inc(S("c_in"), 16)
            n_ada = 0
            for u in range(RING):
                load_unit(sp, u)
            while n_ada < ADA_FIRST + 3:
                load_ada(sp, n_ada)
                n_ada += 1
            u_next = RING
            for u in range(U_PW2):
                sp.wait_ge(lo_ready, u_next - RING + 1)
                load_unit(sp, u_next)
                u_next += 1
                for _k in range(ADA_PW1):
                    load_ada(sp, n_ada)
                    n_ada += 1
            while n_ada < N_ADA:
                load_ada(sp, n_ada)
                n_ada += 1

            def plain(to):
                nonlocal u_next
                while u_next < to:
                    sp.wait_ge(lo_ready, u_next - RING + 1)
                    load_unit(sp, u_next)
                    u_next += 1

            for layer in range(2):
                for hf in range(2):
                    u0 = U_FFN[layer] + hf * F_UNITS
                    plain(u0)
                    n = 2 * LOOP_PAIRS
                    with sp.Fori(0, LOOPS) as i:
                        for k in range(n):
                            sp.wait_ge(lo_ready, i * n + (u0 + k - RING + 1))
                            load_unit(sp, u0 + k, shift=i * (LOOP_PAIRS * P))
                    u_next = u0 + LOOPS * n
                    plain(u0 + F_UNITS)
            plain(NU)

        @block.gpsimd
        def _(pool):
            def load_rows(bk):
                n = xi_rows[bk]
                if bk >= 2:
                    pool.wait_ge(S("xi_pe"), bk - 1)
                if bk < 4:
                    src = a["x_prompt"][0, bk * P:(bk + 1) * P, :]
                elif bk == 4:
                    src = a["x_sample"].rearrange("b t d -> (b t) d")
                else:
                    src = a["state_conv"].rearrange("l b t d -> (l b t) d")[120 * (bk - 5):120 * (bk - 4), :]
                pool.dma_start(stage[0:n, bk % 2, :], src).then_inc(S(f"xi_in{bk % 2}"), 16)

            load_rows(0)
            load_rows(1)
            nc.gpsimd.memset(ones[:], 1.0).then_inc(S("const"), 1)
            nc.gpsimd.memset(epst[:], EPS).then_inc(S("const"), 1)
            nc.gpsimd.memset(u_p[:, :, 0:CW - 1], 0.0).then_inc(S("const"), 1)
            for bk in range(2, 7):
                load_rows(bk)
            pool.dma_start(pgt[:], a["page_table"].rearrange("b n -> (b n)").unsqueeze(0)).then_inc(S("pg_in"), 16)
            pool.dma_start(o["conv_sample"][0, :, 0:CW - 1 - NT, :],
                           a["state_conv"][0, :, NT:CW - 1, :]).then_inc(S("thru"), 16)
            pool.dma_start(wss[:, 0:PAST, :], a["state_win"].rearrange("b s t h d -> b s (t h d)")).then_inc(S("thru"), 16)

            ysmp = y[:, :, TP:T].rearrange("p c (b t) -> p c t b", b=NB)
            fs4 = fs[:, :, :].rearrange("p c (t b) -> p c t b", b=NB)

            def bc(col):
                return col.unsqueeze(2).unsqueeze(3).to_broadcast([P, DC, NT, NB])

            pool.wait_ge(tile_free, 2 * DC)
            pool.wait_ge(S("xi_act"), 7)
            pool.wait_ge(S("xi_dve"), 7)
            step = S("convs")
            nc.gpsimd.tensor_tensor(ysmp, u_s[:, :, 0:NT, :], bc(wdT[:, 0:DC]), ALU.mult).then_inc(step, 1)
            pool.wait_ge(step, 1)
            nc.gpsimd.tensor_tensor(ysmp, ysmp, bc(vT[:, R_BDW:R_BDW + DC]), ALU.add).then_inc(step, 1)
            for k in range(1, CW):
                nc.gpsimd.tensor_tensor(fs4, u_s[:, :, k:k + NT, :], bc(wdT[:, k * DC:(k + 1) * DC]),
                                        ALU.mult).then_inc(step, 1)
                pool.wait_ge(step, 2 * k + 1)
                nc.gpsimd.tensor_tensor(ysmp, ysmp, fs4, ALU.add).then_inc(step, 1)
                pool.wait_ge(step, 2 * k + 2)

            pool.wait_ge(tile_done, U_PW2 + 1)
            pool.wait_ge(ada_ev, 2 * N_ADA)
            pool.dma_start(dist[:], c["dist"]).then_inc(S("cb_in"), 16)
            pool.dma_start(w2t[:], a["w_cmp2"].rearrange("t e d -> e t d")).then_inc(S("cb_in"), 16)
            pool.dma_start(distc[:], c["distc"]).then_inc(S("cb_in"), 16)
            pool.dma_start(maskc[:], c["maskc"]).then_inc(S("cb_in"), 16)
            pool.dma_start(tmask[:], c["tmask"]).then_inc(S("cb_in"), 16)
            pool.dma_start(tabc[:], c["tabc"]).then_inc(S("cb_in"), 16)
            pool.dma_start(expd[:], c["expd"]).then_inc(S("cb_in"), 16)

            for tb in range(5):
                pool.wait_ge(S("rt_ev"), 5 * tb + 3)
                if tb < 4:
                    pool.dma_start(kvp[tb], stage[:, tb % 2, :]).then_inc(S(f"kv_out{tb % 2}"), 16)
                    pool.wait_ge(S("rt_ev"), 5 * tb + 5)
                    pool.dma_start(wps[tb], winst[:, tb % 2, :]).then_inc(S(f"kv_out{tb % 2}"), 16)
                else:
                    pool.dma_start(kvs, stage[0:TS, 0, :]).then_inc(S("kv_out0"), 16)
                    pool.wait_ge(S("rt_ev"), 5 * tb + 5)
                    for b in range(NB):
                        pool.dma_start(wss[b, PAST:PAST + NT, :], winst[NT * b:NT * b + NT, 0, :]).then_inc(S("win_out"), 16)
            pool.wait_ge(S("kv_out0"), 16 * 5)
            pool.wait_ge(S("kv_out1"), 16 * 4)
            pool.wait_ge(S("win_out"), 16 * NB)
            pool.wait_ge(tile_done, U_WO)
            w1 = a["w_cmp1"].rearrange("t (j l) d e -> t (l d) j e", l=2)
            pool.dma_start(w1k[:], w1[0]).then_inc(S("w1_in"), 16)
            pool.dma_start(w1v[:], w1[1]).then_inc(S("w1_in"), 16)
            pool.wait_ge(S("pg_in"), 16)
            for b in range(NB):
                if b >= 2:
                    pool.wait_ge(S("ct_pe"), b - 1)
                elif b == 1:
                    pool.wait_ge(S("gs_pe"), 2)
                for pg in range(NPG):
                    page = pool.value_load(pgt[0:1, b * NPG + pg:b * NPG + pg + 1], min_val=0,
                                           max_val=a["cache_kv"].shape[0] - 1)
                    n = PG // 2
                    for e in range(2):
                        src = page_rows[bass.ds(page, 1), :, e, 0:512]
                        pool.dma_start(Cb[b % 2][pg * n:(pg + 1) * n, :, e, :],
                                       src.rearrange("n q (h d) -> (n q) h d", d=HD)).then_inc(S(f"cc_in{b % 2}"), 16)
            for n in range(4 * NKV):
                L = P * (n % 4 + 1)
                pool.wait_ge(S("pw"), n + 1)
                for s in range(8):
                    nc.gpsimd.tensor_tensor(Pp[:, n % 2, s, 0:L], Pp[:, n % 2, s, 0:L],
                                            wgt[:, n % 2, s:s + 1].to_broadcast([P, L]), ALU.mult).then_inc(S("scaled"), 1)
            pool.wait_ge(S("pt_pe"), 4 * (2 * 10 + 4))
            pool.dma_start(tabs[:], c["tabs"]).then_inc(S("tabs_in"), 16)

            def load_sample(b):
                if b >= 2:
                    pool.wait_ge(S("s_pv"), b - 1)
                for pg in range(NPG):
                    page = pool.value_load(pgt[0:1, b * NPG + pg:b * NPG + pg + 1], min_val=0,
                                           max_val=a["cache_kv"].shape[0] - 1)
                    n = PG // 2
                    pool.dma_start(Cs[pg * n:(pg + 1) * n, b % 2],
                                   page_rows[bass.ds(page, 1), :, :, 512:1024].rearrange("n q e f -> (n q) e f"))\
                        .then_inc(S(f"s_in{b % 2}"), 16)
                pool.dma_start(Cw[:, b % 2], win_rows[b]).then_inc(S(f"s_in{b % 2}"), 16)

            load_sample(0)
            load_sample(1)
            for b in range(NB):
                pool.wait_ge(S("s_wgt"), b + 1)
                for br in range(2):
                    nc.gpsimd.tensor_tensor(Ps[:, b % 2, br, :], Ps[:, b % 2, br, :],
                                            wgt[:, b % 2, 1 + br:2 + br].to_broadcast([P, NKS]),
                                            ALU.mult).then_inc(S("s_scaled"), 1)
                if b + 2 < NB:
                    load_sample(b + 2)
            for tb in range(5):
                n = P if tb < 4 else TS
                pool.wait_ge(S("fe_act"), tb + 1)
                pool.wait_ge(S("fe_dve"), tb + 1)
                dst = o["y_prompt"][0, tb * P:(tb + 1) * P, :] if tb < 4 else o["y_sample"].rearrange("b t d -> (b t) d")
                pool.dma_start(dst, stage[0:n, tb % 2, :]).then_inc(S(f"y_out{tb % 2}"), 16)
            pool.wait_ge(S("y_out0"), 48)
            pool.wait_ge(S("y_out1"), 32)
            pool.wait_ge(S("thru"), 32)

        @block.scalar
        def _(act):
            A = nc.scalar.activation

            def split_hi(u, ub=None):
                if u >= NU:
                    return
                K, w = UNITS[u][2], UNITS[u][4]
                if ub is None:
                    act.wait_ge(raw_in[u % RING], 16 * (u // RING + 1))
                    if u >= RING:
                        act.wait_ge(tile_done, u - RING + 1)
                else:
                    i, n = ub
                    act.wait_ge(raw_in[u % RING], i * (16 * n // RING) + 16 * (u // RING + 1))
                    act.wait_ge(tile_done, i * n + (u - RING + 1))
                A(wh[:, u % RING, 0:K, 0:w], raw[:, u % RING, 0:K, 0:w], ACT.Copy).then_inc(hi_ready, 1)

            def ada_out(n):
                for k in range(2):
                    act.wait_ge(ada_used, n + 1)
                    q = 2 * n + k
                    A(mods[:, q, :], ps[:, 6 + n % 2, k * 16:k * 16 + 9], ACT.Identity,
                      bias=badaT[:, q:q + 1]).then_inc(ada_ev, 1)

            def squares(st, ready, count):
                for s, v in zip(ready, count):
                    act.wait_ge(s, v)
                for cc in range(DC):
                    A(sqb[:, cc, :], x[:, cc, :], ACT.Square).then_inc(S("st_sq"), 1)
                act.wait_ge(S("st_ss"), st + 1)
                A(halves(r[:]), stats, ACT.Sqrt, scale=1.0 / D, bias=epst[:]).then_inc(S("st_rms"), 1)

            def norm_hi(k):
                sh = NORMS[k][1]
                if k == 3:
                    act.wait_ge(tile_done, U_IN)
                if k < 5:
                    act.wait_ge(S("n_s"), 3 * k + 3)
                    A(Hh[:, :, TP:T], fs[:], ACT.Copy).then_inc(S("n_hi"), 1)
                for cc in range(DC):
                    act.wait_ge(S("n_t"), DC * k + cc + 1)
                    dst = Hh if k < 5 else xf
                    A(dst[:, cc, 0:TP], t2[:, cc % 2, 0:TP], ACT.Identity,
                      bias=mods[:, sh * DC + cc, 0:1]).then_inc(S("n_hi"), 1)

            act.wait_ge(S("c_in"), 32)
            A(rows0[0:72, 4, :], rows0[0:72, 4, :], ACT.Silu).then_inc(S("c_silu"), 1)
            split_hi(0)
            split_hi(1)
            act.wait_ge(S("vec_pe"), 2)
            A(cT[:], ps[:, 6, 0:72], ACT.Copy).then_inc(S("vec_act"), 1)
            for bk in range(7):
                act.wait_ge(S("xi_pe"), bk + 1)
                n = xi_rows[bk]
                src = ps[:, 2 * (bk % 3) + 1, 0:4 * n].rearrange("p (c t) -> p c t", c=4)
                if bk < 5:
                    dst = x[:, 4:8, bk * P:bk * P + n]
                else:
                    dst = u_s[:, 4:8, 0:CW - 1, 4 * (bk - 5):4 * (bk - 4)].rearrange("p c t b -> p c b t")
                    src = src.rearrange("p c (b t) -> p c b t", b=4)
                A(dst, src, ACT.Copy).then_inc(S("xi_act"), 1)
            squares(0, [S("xi_dve"), S("xi_act"), S("const")], [5, 5, 3])
            for n in range(ADA_FIRST):
                ada_out(n)
            norm_hi(0)

            n_ada = ADA_FIRST
            for j in range(DC):
                for k in range(2):
                    u = 2 * j + k
                    split_hi(u + SPLIT_AHEAD)
                    if k == 1:
                        act.wait_ge(tile_done, u + 1)
                        if j >= 2:
                            act.wait_ge(tile_free, 2 * (j - 1))
                        else:
                            act.wait_ge(S("n_lo"), 9)
                        A(halves(t2[:, j % 2, :]), tile(u), ACT.Sigmoid,
                          bias=vT[:, R_B1 + DC + j:R_B1 + DC + j + 1]).then_inc(S("sig"), 1)
                    for _k in range(ADA_PW1):
                        ada_out(n_ada)
                        n_ada += 1
            act.wait_ge(S("cr_pe"), 1)
            A(stage[0:CW - 1, 0, :].rearrange("p (b f) -> p b f", b=2), ps[0:CW - 1, 0:2, :], ACT.Copy).then_inc(S("cr_ev"), 1)
            A(stage[0:TS, 1, :].rearrange("p (b f) -> p b f", b=2), ps[0:TS, 2:4, :], ACT.Copy).then_inc(S("cr_ev"), 1)
            act.wait_ge(S("cr_ev"), 2)
            act.dma_start(o["conv_prompt"][0, 0], stage[0:CW - 1, 0, :]).then_inc(S("cr_out"), 16)
            for t in range(NT):
                act.dma_start(o["conv_sample"][0, :, CW - 1 - NT + t, :], stage[NB * t:NB * t + NB, 1, :]).then_inc(S("cr_out"), 16)
            while n_ada < N_ADA:
                ada_out(n_ada)
                n_ada += 1

            act.wait_ge(S("ln_pe"), 1)
            A(halves(mu[:]), stats, ACT.Copy, scale=1.0 / D).then_inc(S("ln_mu"), 1)
            for cc in range(DC):
                act.wait_ge(S("ln_yc"), cc + 1)
                A(sqb[:, cc, :], y[:, cc, :], ACT.Square).then_inc(S("ln_sq"), 1)
            act.wait_ge(S("ln_pe"), 2)
            A(halves(r[:]), stats, ACT.Sqrt, scale=1.0 / D, bias=epst[:]).then_inc(S("ln_rms"), 1)
            for cc in range(DC):
                act.wait_ge(S("ln_t"), cc + 1)
                A(y[:, cc, :], t2[:, cc % 2, :], ACT.Silu, scale=vT[:, R_LNG + cc:R_LNG + cc + 1],
                  bias=vT[:, R_LNB + cc:R_LNB + cc + 1]).then_inc(S("ln_s"), 1)
                act.wait_ge(S("ln_s"), cc + 1)
                A(Hh[:, cc, :], y[:, cc, :], ACT.Copy).then_inc(S("ln_hi"), 1)
            for u in range(U_PW2, U_FFN[0]):
                split_hi(u + SPLIT_AHEAD)

            def ffn(layer):
                act.wait_ge(S("n_lo"), 9 * (2 if layer == 0 else 5))
                for hf in range(2):
                    u0 = U_FFN[layer] + hf * F_UNITS
                    q0 = (2 * layer + hf) * FHC

                    def pair(p, i=None):
                        n, q = 2 * LOOP_PAIRS, q0 + p
                        more = 0 if i is None else i * LOOP_PAIRS
                        for k in range(2):
                            split_hi(u0 + 2 * p + k + SPLIT_AHEAD, None if i is None else (i, n))
                        act.wait_ge(tile_done, (0 if i is None else i * n) + (u0 + 2 * p + 1))
                        if q >= 2:
                            act.wait_ge(S("ff_lo"), more + (q - 1))
                        A(halves(t2[:, q % 2, :]) if i is None else halves(t2s(q, i)), tile(u0 + 2 * p), ACT.Silu)\
                            .then_inc(S("ff_silu"), 1)

                    def high(p, i=None):
                        q = q0 + p
                        more = 0 if i is None else i * LOOP_PAIRS
                        act.wait_ge(tile_free, (0 if i is None else i * 2 * LOOP_PAIRS) + (u0 + 2 * p + 2))
                        A(ah[:, p, :] if i is None else ah[:, bass.ds(i * LOOP_PAIRS + p, 1), :].rearrange("p a t -> p (a t)"),
                          t2[:, q % 2, :] if i is None else t2s(q, i), ACT.Copy).then_inc(S("ff_hi"), 1)

                    def t2s(q, i):
                        return t2[:, bass.ds((i + q) % 2, 1), :].rearrange("p a t -> p (a t)")

                    for p in range(FHC):
                        pair(p)
                        high(p)
                    for m in range(DC):
                        split_hi(u0 + 2 * FHC + m + SPLIT_AHEAD)

            squares(1, [x_upd], [8])
            norm_hi(1)
            ffn(0)
            squares(2, [x_upd], [24])
            norm_hi(2)
            for u in range(U_KV, U_IN):
                split_hi(u + SPLIT_AHEAD)
            def rows_out(tb):
                n = P if tb < 4 else TS
                for g3 in range(3):
                    k = 3 * tb + g3
                    act.wait_ge(S("rt_pe"), k + 1)
                    src = ps[0:n, 6 + k % 2, :]
                    if g3 == 0 and tb >= 2:
                        act.wait_ge(S(f"kv_out{tb % 2}"), 32 * (tb // 2))
                    if g3 == 0 and tb == 0:
                        act.wait_ge(S("cr_out"), 16 * (1 + NT))
                    dst = stage[0:n, tb % 2, 512 * g3:512 * g3 + 512] if g3 < 2 else winst[0:n, tb % 2, :]
                    A(dst, src, ACT.Copy).then_inc(S("rt_ev"), 1)
                    if g3:
                        A(vrow[0:n, tb, g3 - 1].rearrange("p h d -> p (h d)"), src[:, 256:512], ACT.Copy).then_inc(S("rt_ev"), 1)
            norm_hi(3)
            for tb in range(5):
                rows_out(tb)
            for t in range(DC):
                u = U_IN + t
                split_hi(u + SPLIT_AHEAD)
                act.wait_ge(tile_done, u + 1)
                kv = t // 2
                A(halves(qT[64 * (kv % 2):64 * (kv % 2) + 64, (kv // 2) * 4 + 2 * (t % 2), :]), tile(u)[0:64],
                  ACT.Copy, scale=-SCALE).then_inc(S("q_act"), 1)
                A(qs[64 * (kv % 2):64 * (kv % 2) + 64, kv // 2, :, 2 * (t % 2), :], smp_cols(tile(u)[0:64]),
                  ACT.Copy, scale=-SCALE).then_inc(S("q_act"), 1)
            u = U_IN + DC
            split_hi(u + SPLIT_AHEAD)
            act.wait_ge(tile_free, u + 1)
            A(t2[0:3 * NH, 0, :], t2[0:3 * NH, 0, :], ACT.Sigmoid).then_inc(S("q_act"), 1)
            act.wait_ge(S("gs_pe"), 1)
            A(gates[:].rearrange("p i h r -> p i (h r)"),
              ps[:, 6, 0:4 * 48].rearrange("p (i f) -> p i f", i=4), ACT.Copy).then_inc(S("gates"), 1)

            act.wait_ge(S("hp_pe"), 1)
            A(peb[:], ps[:, 6, 0:2], ACT.Copy).then_inc(S("hc"), 1)
            act.wait_ge(S("hc"), 1)
            act.wait_ge(S("gs_dve"), 2)
            for t in range(2):
                act.wait_ge(S("hp_pe"), 2 + t)
                A(t2[:, 0, P * t:P * t + G * NCP], ps[:, t, 0:G * NCP], ACT.Silu, bias=peb[:, t:t + 1]).then_inc(S("hc"), 1)
            for g2 in range(2):
                for bb in range(4):
                    b = 4 * g2 + bb
                    act.wait_ge(S("ct_pe"), b + 1)
                    if bb == 0 and g2 == 1:
                        act.wait_ge(S("hs_pe"), 2)
                    A(CPv[:, bb].rearrange("p h q -> p (h q)"), ps[:, 5, :], ACT.Copy).then_inc(S("cp_act"), 1)
                for t in range(2):
                    act.wait_ge(S("hs_pe"), 2 * g2 + t + 1)
                    n = 4 * NKV * NCS
                    if t == 0 and g2 == 1:
                        act.wait_ge(S("kc_pe"), 3)
                    dst = t2[:, 1, 0:n] if t == 0 else hv_s[:, g2 * n:(g2 + 1) * n]
                    A(dst, ps[:, t, 0:n], ACT.Silu, bias=peb[:, t:t + 1]).then_inc(S("hc"), 1)

            def exps(n):
                L = P * (n % 4 + 1)
                for s in range(8):
                    act.wait_ge(S("sc"), 9 * n + s + 1)
                    A(Pp[:, n % 2, s, 0:L], Pp[:, n % 2, s, 0:L], ACT.Exp, scale=-1.0, bias=nmin[:, n % 2, s:s + 1],
                      accum_out=sums[:, n % 2, s:s + 1]).then_inc(S("pexp"), 1)
                act.wait_ge(S("zc"), 2 * n + 2)
                A(Pc[:, n % 2], Pc[:, n % 2], ACT.Exp, scale=-1.0).then_inc(S("pexp"), 1)

            for n in range(4 * NKV + 1):
                if n < 4 * NKV:
                    exps(n)
                if n >= 1:
                    m = n - 1
                    for j in range(pt0[m], pt0[m + 1]):
                        if j % 2:
                            act.wait_ge(S("pt_pe"), j + 1)
                            act.wait_ge(S("pv"), j - 1)
                            K = NCP if j == pt0[m + 1] - 1 else P
                            A(PT[0:K, 1, :], ps[0:K, 5, :], ACT.Copy).then_inc(S("pt_act"), 1)
                    if m % 2:
                        act.wait_ge(S("pv"), pt0[m + 1])
                        kv, i = m // 4, m % 4
                        src = ps[0:HD, 7, :].rearrange("p (g q) -> p g q", g=G)
                        for par in range(2):
                            A(oT[64 * par:64 * par + 64, 2 * kv:2 * kv + 2, P * i:P * i + P], src[:, par::2, :], ACT.Copy)\
                                .then_inc(S("o_act"), 1)

            for b in range(NB + 1):
                if b < NB:
                    act.wait_ge(S("kt_pe"), b + 1)
                    if b >= 1:
                        act.wait_ge(S("s_sc"), b)
                    A(KT[:, 1], ps[:, 5, :].rearrange("p (a e q) -> p a e q", a=2, e=2), ACT.Copy).then_inc(S("kt_act"), 1)
                    for br in range(2):
                        act.wait_ge(S("s_z"), 5 * b + br + 1)
                        A(Ps[:, b % 2, br, :], Ps[:, b % 2, br, :], ACT.Exp, scale=-1.0, bias=nmin[:, b % 2, 1 + br:2 + br],
                          accum_out=sums[:, b % 2, 1 + br:2 + br]).then_inc(S("s_exp"), 1)
                    act.wait_ge(S("s_z"), 5 * b + 4)
                    A(Pcs[:, b % 2, 0:NCS], Pcs[:, b % 2, 0:NCS], ACT.Exp, scale=-1.0, bias=nmin[:, b % 2, 0:1],
                      accum_out=sums[:, b % 2, 0:1]).then_inc(S("s_exp"), 1)
                if b >= 1:
                    m = b - 1
                    act.wait_ge(S("s_pt"), m + 1)
                    act.wait_ge(S("s_pv"), m) if m else None
                    A(PTs[:, 3:5].rearrange("p a q -> p (a q)"), ps[:, 7, 0:256], ACT.Copy).then_inc(S("s_pta"), 1)
                    A(PTs[0:TS, 5], ps[0:TS, 7, 256:384], ACT.Copy).then_inc(S("s_pta"), 1)
            act.wait_ge(S("o_dve"), 4 * NKV + 2 * NB)
            act.wait_ge(S("s_pv"), NB)
            for cc in range(DC):
                A(Hh[:, cc, :], oT[:, cc, :], ACT.Copy).then_inc(S("oh"), 1)
            for u in range(U_WO, U_FFN[1]):
                split_hi(u + SPLIT_AHEAD)
            squares(3, [x_upd], [32])
            norm_hi(4)
            ffn(1)
            squares(4, [x_upd], [48])
            norm_hi(5)
            for tb in range(5):
                n = P if tb < 4 else TS
                act.wait_ge(S("f_pe"), tb + 1)
                if tb >= 2:
                    act.wait_ge(S(f"y_out{tb % 2}"), 16 * (tb // 2))
                A(stage[0:n, tb % 2, 512:1024], ps[0:n, 2 * (tb % 3) + 1, :], ACT.Copy).then_inc(S("fe_act"), 1)

        @block.vector
        def _(dve):
            V = nc.vector

            def split_lo(u):
                if u >= NU:
                    return
                K, w = UNITS[u][2], UNITS[u][4]
                dve.wait_ge(hi_ready, u + 1)
                V.tensor_tensor(wl[:, u % RING, 0:K, 0:w], raw[:, u % RING, 0:K, 0:w],
                                wh[:, u % RING, 0:K, 0:w].bitcast(F32), ALU.subtract).then_inc(lo_ready, 1)

            def norm(k):
                g0, sh, sc = NORMS[k]
                dve.wait_ge(ada_ev, 2 * max(4 * (sh + 1), 4 * (sc + 1)))
                V.scalar_tensor_tensor(acoef[:], mods[:, sc * DC:(sc + 1) * DC, :], 1.0,
                                       vT[:, g0:g0 + DC].unsqueeze(2).to_broadcast([P, DC, 1 + NB]),
                                       ALU.add, ALU.mult).then_inc(S("n_a"), 1)
                if k != 3:
                    dve.wait_ge(S("st_rms"), STAT_OF[k] + 1)
                    V.reciprocal(r[:], r[:]).then_inc(S("st_r"), 1)
                    dve.wait_ge(S("st_r"), STAT_OF[k] + 1)
                dve.wait_ge(S("n_a"), k + 1)
                f4 = fs[:].rearrange("p c (b t) -> p c b t", b=NB)
                if k == 5:
                    f4 = xf[:, :, TP:T].rearrange("p c (b t) -> p c b t", b=NB)
                f3 = fs[:] if k < 5 else xf[:, :, TP:T]

                def per_seq(ap):
                    return ap.unsqueeze(3).to_broadcast([P, DC, NB, NT])

                if k >= 1:
                    dve.wait_ge(S("convs"), 2 * CW)
                V.tensor_tensor(f4, x[:, :, TP:T].rearrange("p c (b t) -> p c b t", b=NB), per_seq(acoef[:, :, 1:]),
                                ALU.mult).then_inc(S("n_s"), 1)
                dve.wait_ge(S("n_s"), 3 * k + 1)
                V.tensor_tensor(f3, f3, r[:, TP:T].unsqueeze(1).to_broadcast([P, DC, TS]), ALU.mult).then_inc(S("n_s"), 1)
                dve.wait_ge(S("n_s"), 3 * k + 2)
                V.tensor_tensor(f4, f4, per_seq(mods[:, sh * DC:(sh + 1) * DC, 1:]), ALU.add).then_inc(S("n_s"), 1)

                def scaled(cc):
                    if cc >= 2:
                        dve.wait_ge(*((S("n_hi"), 9 * 5 + cc - 1) if k == 5 else (S("n_lo"), 9 * k + cc)))
                    V.scalar_tensor_tensor(t2[:, cc % 2, 0:TP], x[:, cc, 0:TP], acoef[:, cc, 0:1], r[:, 0:TP],
                                           ALU.mult, ALU.mult).then_inc(S("n_t"), 1)

                def low(cc):
                    dve.wait_ge(S("n_hi"), 9 * k + cc + 2)
                    V.scalar_tensor_tensor(Hl[:, cc, 0:TP], t2[:, cc % 2, 0:TP], mods[:, sh * DC + cc, 0:1],
                                           Hh[:, cc, 0:TP].bitcast(F32), ALU.add, ALU.subtract).then_inc(S("n_lo"), 1)

                scaled(0)
                scaled(1)
                if k < 5:
                    dve.wait_ge(S("n_hi"), 9 * k + 1)
                    V.tensor_tensor(Hl[:, :, TP:T], fs[:], Hh[:, :, TP:T].bitcast(F32), ALU.subtract).then_inc(S("n_lo"), 1)
                for cc in range(DC):
                    if k < 5:
                        low(cc)
                    if cc + 2 < DC:
                        scaled(cc + 2)

            def residual(rs, m, u):
                g = GATES[rs] * DC + m
                t = tile(u)
                dve.wait_ge(tile_done, u + 1)
                dve.wait_ge(x_upd, DC * rs + max(m - 1, 0))
                V.tensor_tensor(rtmp[:, m % 2, :].rearrange("p (b t) -> p b t", b=NB),
                                t[:, 1, HT - TS:HT].rearrange("p (b t) -> p b t", b=NB),
                                mods[:, g, 1:].unsqueeze(2).to_broadcast([P, NB, NT]), ALU.mult).then_inc(S("r_s"), 1)
                V.scalar_tensor_tensor(x[:, m, 0:HT], t[:, 0, :], mods[:, g, 0:1], x[:, m, 0:HT],
                                       ALU.mult, ALU.add).then_inc(S("r_p"), 1)
                V.scalar_tensor_tensor(x[:, m, HT:TP], t[:, 1, 0:TP - HT], mods[:, g, 0:1], x[:, m, HT:TP],
                                       ALU.mult, ALU.add).then_inc(tile_free, 1)
                dve.wait_ge(S("r_s"), DC * rs + m + 1)
                V.tensor_tensor(x[:, m, TP:T], x[:, m, TP:T], rtmp[:, m % 2, :], ALU.add).then_inc(x_upd, 1)

            dve.wait_ge(S("vec_pe"), 1)
            V.tensor_copy(vT[:], ps[:, 7, 0:R_END]).then_inc(S("vec_dve"), 1)
            V.tensor_copy(wdT[:], ps[:, 7, R_END:R_END + 248]).then_inc(S("vec_dve"), 1)
            V.tensor_copy(badaT[:], ps[:, 7, 384:512]).then_inc(S("vec_dve"), 1)
            split_lo(0)
            split_lo(1)
            for bk in range(7):
                dve.wait_ge(S("xi_pe"), bk + 1)
                n = xi_rows[bk]
                src = ps[:, 2 * (bk % 3), 0:4 * n].rearrange("p (c t) -> p c t", c=4)
                if bk < 5:
                    dst = x[:, 0:4, bk * P:bk * P + n]
                else:
                    dst = u_s[:, 0:4, 0:CW - 1, 4 * (bk - 5):4 * (bk - 4)].rearrange("p c t b -> p c b t")
                    src = src.rearrange("p c (b t) -> p c b t", b=4)
                V.tensor_copy(dst, src).then_inc(S("xi_dve"), 1)
            dve.wait_ge(S("vec_dve"), 3)
            dve.wait_ge(S("xi_act"), 5)
            dve.wait_ge(S("xi_dve"), 5)
            norm(0)

            dve.wait_ge(S("const"), 3)
            taps = S("conv")
            for j in range(DC):
                ua = 2 * j
                split_lo(ua + SPLIT_AHEAD)
                split_lo(ua + 1 + SPLIT_AHEAD)
                dve.wait_ge(S("sig"), j + 1)
                ta, sg, b1 = tile(ua), t2[:, j % 2, :], vT[:, R_B1 + j:R_B1 + j + 1]
                n0 = CW - 1
                V.scalar_tensor_tensor(u_p[:, j, n0:n0 + HT], ta[:, 0, :], b1, sg[:, 0:HT], ALU.add, ALU.mult).then_inc(S("glu_p"), 1)
                V.scalar_tensor_tensor(u_p[:, j, n0 + HT:n0 + TP], ta[:, 1, 0:TP - HT], b1, sg[:, HT:TP],
                                       ALU.add, ALU.mult).then_inc(S("glu_p"), 1)
                V.scalar_tensor_tensor(u_s[:, j, n0:, :].rearrange("p t b -> p b t"), ta[:, 1, TP - HT:HT].rearrange("p (b t) -> p b t", b=NB), b1,
                                       sg[:, TP:T].rearrange("p (b t) -> p b t", b=NB), ALU.add, ALU.mult).then_inc(tile_free, 2)
                dve.wait_ge(S("glu_p"), 2 * (j + 1))
                acc = y[:, j, 0:TP]
                V.tensor_scalar(acc, u_p[:, j, 0:TP], wdT[:, j:j + 1], vT[:, R_BDW + j:R_BDW + j + 1],
                                ALU.mult, ALU.add).then_inc(taps, 1)
                per = 6
                with dve.Fori(0, (CW - 1) // per) as i:
                    for k in range(1, per + 1):
                        dve.wait_ge(taps, i * per + (CW * j + k))
                        V.scalar_tensor_tensor(acc, u_p[:, j, bass.ds(i * per + k, TP)],
                                               wdT[:, bass.ds(i * (per * DC) + (k * DC + j), 1)], acc,
                                               ALU.mult, ALU.add).then_inc(taps, 1)

            dve.wait_ge(S("ln_mu"), 1)
            dve.wait_ge(S("convs"), 2 * CW)
            dve.wait_ge(taps, CW * DC)
            for cc in range(DC):
                V.tensor_tensor(y[:, cc, :], y[:, cc, :], mu[:], ALU.subtract).then_inc(S("ln_yc"), 1)
            dve.wait_ge(S("ln_rms"), 1)
            V.reciprocal(r[:], r[:]).then_inc(S("ln_r"), 1)
            dve.wait_ge(S("ln_r"), 1)
            dve.wait_ge(S("ln_yc"), DC)

            def ln_t(cc):
                if cc >= 2:
                    dve.wait_ge(S("ln_s"), cc - 1)
                V.tensor_tensor(t2[:, cc % 2, :], y[:, cc, :], r[:], ALU.mult).then_inc(S("ln_t"), 1)

            ln_t(0)
            ln_t(1)
            for cc in range(DC):
                if cc + 2 < DC:
                    ln_t(cc + 2)
                dve.wait_ge(S("ln_hi"), cc + 1)
                V.tensor_tensor(Hl[:, cc, :], y[:, cc, :], Hh[:, cc, :].bitcast(F32), ALU.subtract).then_inc(S("ln_lo"), 1)
            for m in range(DC):
                split_lo(U_PW2 + m + SPLIT_AHEAD)
                residual(0, m, U_PW2 + m)

            def ffn(layer):
                for hf in range(2):
                    u0 = U_FFN[layer] + hf * F_UNITS
                    q0 = (2 * layer + hf) * FHC
                    for p in range(FHC):
                        q = q0 + p
                        for k in range(2):
                            split_lo(u0 + 2 * p + k + SPLIT_AHEAD)
                        dve.wait_ge(tile_done, u0 + 2 * p + 2)
                        dve.wait_ge(S("ff_silu"), q + 1)
                        t = halves(t2[:, q % 2, :])
                        V.tensor_tensor(t, tile(u0 + 2 * p + 1), t, ALU.mult).then_inc(tile_free, 2)
                        dve.wait_ge(S("ff_hi"), q + 1)
                        V.tensor_tensor(al[:, p, :], t2[:, q % 2, :], ah[:, p, :].bitcast(F32), ALU.subtract).then_inc(S("ff_lo"), 1)
                    dve.wait_ge(x_upd, DC * (1 + 3 * layer + hf))
                    for m in range(DC):
                        u = u0 + 2 * FHC + m
                        split_lo(u + SPLIT_AHEAD)
                        residual(1 + 3 * layer + hf, m, u)

            dve.wait_ge(x_upd, 8)
            norm(1)
            ffn(0)
            dve.wait_ge(x_upd, 24)
            norm(2)
            dve.wait_ge(S("n_lo"), 27)
            for f in range(12):
                u = U_KV + f
                split_lo(u + SPLIT_AHEAD)
                dve.wait_ge(tile_done, u + 1)
                V.tensor_copy(halves(kvT[:, KV_SLOT[f], :]), tile(u)).then_inc(tile_free, 1)
            dve.wait_ge(tile_free, U_IN)
            norm(3)
            for t in range(DC):
                u = U_IN + t
                split_lo(u + SPLIT_AHEAD)
                dve.wait_ge(S("q_act"), 2 * (t + 1))
                kv = t // 2
                V.tensor_scalar(qs[64 * (kv % 2):64 * (kv % 2) + 64, kv // 2, :, 2 * (t % 2) + 1, :],
                                smp_cols(tile(u)[64:128]), -SCALE, None, ALU.mult).then_inc(S("q_dve"), 1)
                V.tensor_scalar(halves(qT[64 * (kv % 2):64 * (kv % 2) + 64, (kv // 2) * 4 + 2 * (t % 2) + 1, :]),
                                tile(u)[64:128], -SCALE, None, ALU.mult).then_inc(tile_free, 1)
            u = U_IN + DC
            split_lo(u + SPLIT_AHEAD)
            dve.wait_ge(tile_done, u + 1)
            dve.wait_ge(tile_free, u)
            V.tensor_copy(halves(t2[0:3 * NH, 0, :]), tile(u, 3 * NH)).then_inc(tile_free, 1)
            dve.wait_ge(tile_free, u + 1)
            dve.wait_ge(S("gs_pe"), 2)
            dve.wait_ge(S("cb_in"), 16 * 7)
            tm = t2[:, 1, 0:3 * TS].rearrange("p (f t) -> p f t", t=NT)
            V.tensor_tensor(tm, ps[:, 7, 0:3 * TS].rearrange("p (f t) -> p f t", t=NT),
                            tmask[:].unsqueeze(1).to_broadcast([P, 3 * NB, NT]), ALU.mult).then_inc(S("gs_dve"), 1)
            dve.wait_ge(S("gs_dve"), 1)
            V.reduce_sum(gs[:].rearrange("p a b -> p (a b)"), tm, AX.X).then_inc(S("gs_dve"), 1)

            dve.wait_ge(tile_free, U_WO)
            dve.wait_ge(S("rt_pe"), 15)
            for th in range(2 * NKV):
                for par in range(2):
                    src = kvT[64 * (th % 2):64 * (th % 2) + 64, KV_SLOT[th // 2], par:TP:2]
                    V.tensor_copy(P2[64 * par:64 * par + 64, th, :], src).then_inc(S("p2"), 1)
            dve.wait_ge(S("kc_pe"), 1)
            for par in range(2):
                V.tensor_copy(kcT_p[64 * par:64 * par + 64, :, :],
                              ps[0:64, 2, 0:G * NCP].rearrange("p (h n) -> p h n", n=NCP)[:, par::2, :]).then_inc(S("kc_dve"), 1)
            dve.wait_ge(S("kc_pe"), 2)
            V.tensor_copy(vc_p[0:NCP].rearrange("p h d -> p (h d)"), ps[0:NCP, 3, 0:NKV * HD]).then_inc(S("kc_dve"), 1)
            for g2 in range(2):
                for bb in range(4):
                    dve.wait_ge(S("ct_pe"), 4 * g2 + bb + 1)
                    if g2 == 1 and bb == 0:
                        dve.wait_ge(S("hs_pe"), 1)
                    V.tensor_copy(CPk[:, bb].rearrange("p h q -> p (h q)"), ps[:, 4, :]).then_inc(S("cp_dve"), 1)
                dve.wait_ge(S("kc_pe"), 3 + g2)
                src = ps[0:64, 2, 0:4 * NKV * NCS].rearrange("p (b h n) -> p h b n", b=4, h=NKV)
                for par in range(2):
                    V.tensor_copy(kcT_s[64 * par:64 * par + 64, :, 4 * g2:4 * g2 + 4, :], src[:, par::2]).then_inc(S("kc_dve"), 1)

            def scores(n):
                kv, i = n // 4, n % 4
                L = P * (i + 1)
                if i == 0:
                    if kv:
                        dve.wait_ge(S("sc"), 9 * n)
                    for g in range(G):
                        V.tensor_scalar(bias[:, g, :], dist[:], SLOPES[G * kv + g], None, ALU.mult).then_inc(S("bias"), 1)
                    dve.wait_ge(S("bias"), G * (kv + 1))
                if n >= 2:
                    dve.wait_ge(S("pt_pe"), pt0[n - 1])
                for s in range(8):
                    k = 9 * n + s
                    dve.wait_ge(S("sc_pe"), k + 1)
                    V.tensor_tensor_reduce(out=Pp[:, n % 2, s, 0:L], in0=ps[:, k % 4, 0:L], in1=bias[:, s // 2, TP - L:TP],
                                           scale=1.0, scalar=3.0e38, op0=ALU.add, op1=ALU.min,
                                           accum_out=nmin[:, n % 2, s:s + 1]).then_inc(S("sc"), 1)
                k = 9 * n + 8
                dve.wait_ge(S("sc_pe"), k + 1)
                z = Pc[:, n % 2]
                for g in range(G):
                    V.scalar_tensor_tensor(z[:, g, :], distc[:, i, :], SLOPES[G * kv + g], ps[:, k % 4, g * NCP:(g + 1) * NCP],
                                           ALU.mult, ALU.add).then_inc(S("zg") if g < 3 else S("sc"), 1)
                dve.wait_ge(S("zg"), 3 * (n + 1))
                dve.wait_ge(S("sc"), 9 * (n + 1))
                V.tensor_reduce(nmin[:, n % 2, 8:12], z, AX.X, ALU.min).then_inc(S("zc"), 1)
                dve.wait_ge(S("zc"), 2 * n + 1)
                V.tensor_tensor(z, z, nmin[:, n % 2, 8:12].unsqueeze(2).to_broadcast([P, G, NCP]), ALU.subtract).then_inc(S("zc"), 1)

            def weights(n):
                kv, i = n // 4, n % 4
                z, W = Pc[:, n % 2], S("wg")
                dve.wait_ge(S("pexp"), 9 * (n + 1))
                V.tensor_reduce(sums[:, n % 2, 8:12], z, AX.X, ALU.add).then_inc(W, 1)
                dve.wait_ge(W, 4 * n + 1)
                V.reciprocal(wgt[:, n % 2, :], sums[:, n % 2, :]).then_inc(W, 1)
                dve.wait_ge(W, 4 * n + 2)
                w8 = wgt[:, n % 2, 0:8].rearrange("p (g r) -> p g r", r=2)
                V.tensor_tensor(wgt[:, n % 2, 8:12], wgt[:, n % 2, 8:12], gates[:, i, G * kv:G * kv + G, 0], ALU.mult).then_inc(W, 1)
                V.tensor_tensor(w8, w8, gates[:, i, G * kv:G * kv + G, 1:3], ALU.mult).then_inc(S("pw"), 1)
                if i == 0:
                    V.tensor_tensor(z, z, maskc[:].unsqueeze(1).to_broadcast([P, G, NCP]), ALU.mult).then_inc(S("zmask"), 1)
                    dve.wait_ge(S("zmask"), kv + 1)
                dve.wait_ge(W, 4 * n + 3)
                V.tensor_tensor(z, z, wgt[:, n % 2, 8:12].unsqueeze(2).to_broadcast([P, G, NCP]), ALU.mult).then_inc(W, 1)

            def blocks(m):
                for j in range(pt0[m], pt0[m + 1]):
                    if j % 2 == 0:
                        dve.wait_ge(S("pt_pe"), j + 1)
                        if j >= 2:
                            dve.wait_ge(S("pv"), j - 1)
                        K = NCP if j == pt0[m + 1] - 1 else P
                        V.tensor_copy(PT[0:K, 0, :], ps[0:K, 4, :]).then_inc(S("pt_dve"), 1)
                if m % 2 == 0:
                    dve.wait_ge(S("pv"), pt0[m + 1])
                    kv, i = m // 4, m % 4
                    src = ps[0:HD, 6, :].rearrange("p (g q) -> p g q", g=G)
                    for par in range(2):
                        V.tensor_copy(oT[64 * par:64 * par + 64, 2 * kv:2 * kv + 2, P * i:P * i + P], src[:, par::2, :])\
                            .then_inc(S("o_dve"), 1)

            dve.wait_ge(S("gates"), 1)
            dve.wait_ge(S("hs_pe"), 4)
            for n in range(4 * NKV + 1):
                if n < 4 * NKV:
                    scores(n)
                if n >= 1:
                    blocks(n - 1)
                if n < 4 * NKV:
                    weights(n)

            dve.wait_ge(S("vc_pe"), 1)
            V.tensor_copy(vc_s[:].rearrange("p (a e) h d -> p a (e h d)", e=2), ps[0:NCS, 0:4, :]).then_inc(S("vc_dve"), 1)
            for b in range(NB + 1):
                if b < NB:
                    dve.wait_ge(S("kt_pe"), b + 1)
                    if b >= 1:
                        dve.wait_ge(S("s_sc"), b)
                    V.tensor_copy(KT[:, 0], ps[:, 4, :].rearrange("p (a e q) -> p a e q", a=2, e=2)).then_inc(S("kt_dve"), 1)
                    dve.wait_ge(S("s_sc"), b + 1)
                    if b == 0:
                        dve.wait_ge(S("tabs_in"), 16)
                    if b >= 2:
                        dve.wait_ge(S("s_pt"), b - 1)
                    bank, nm = 2 * (b % 2), nmin[:, b % 2, :]
                    for br in range(2):
                        V.tensor_tensor_reduce(out=Ps[:, b % 2, br, :], in0=ps[:, bank + br, 0:NKS], in1=tabs[:, b, :],
                                               scale=1.0, scalar=3.0e38, op0=ALU.add, op1=ALU.min,
                                               accum_out=nm[:, 1 + br:2 + br]).then_inc(S("s_z"), 1)
                    z = Pcs[:, b % 2, 0:NCS]
                    V.tensor_tensor(z, ps[:, bank, NKS:NKS + NCS], tabc[:], ALU.add).then_inc(S("s_z"), 1)
                    dve.wait_ge(S("s_z"), 5 * b + 3)
                    V.tensor_reduce(nm[:, 0:1], z, AX.X, ALU.min).then_inc(S("s_z"), 1)
                if b >= 1:
                    m = b - 1
                    dve.wait_ge(S("s_pt"), m + 1)
                    if m:
                        dve.wait_ge(S("s_pv"), m)
                    V.tensor_copy(PTs[:, 0:2].rearrange("p a q -> p (a q)"), ps[:, 6, 0:256]).then_inc(S("s_ptd"), 1)
                    V.tensor_copy(PTs[0:TS, 2], ps[0:TS, 6, 256:384]).then_inc(S("s_ptd"), 1)
                    V.tensor_copy(PTs[0:NCS, 6], ps[0:NCS, 6, 384:512]).then_inc(S("s_ptd"), 1)
                    dve.wait_ge(S("s_pv"), m + 1)
                    src = ps[0:HD, 7, 384:512].rearrange("p (k e t) -> p k e t", e=2, t=NT)
                    for par in range(2):
                        V.tensor_copy(oT[64 * par:64 * par + 64, :, TP + NT * m:TP + NT * m + NT], src[:, :, par, :]).then_inc(S("o_dve"), 1)
                if b < NB:
                    dve.wait_ge(S("s_exp"), 3 * (b + 1))
                    V.reciprocal(wgt[:, b % 2, 0:3], sums[:, b % 2, 0:3]).then_inc(S("s_z"), 1)
                    dve.wait_ge(S("s_z"), 5 * (b + 1))
                    V.tensor_tensor(wgt[:, b % 2, 0:3], wgt[:, b % 2, 0:3], gs[:, :, b], ALU.mult).then_inc(S("s_wgt"), 1)
                    dve.wait_ge(S("s_wgt"), b + 1)
                    z = Pcs[:, b % 2, 0:NCS]
                    V.tensor_scalar(z, z, wgt[:, b % 2, 0:1], None, ALU.mult).then_inc(S("s_pc"), 1)
            for cc in range(DC):
                dve.wait_ge(S("oh"), cc + 1)
                V.tensor_tensor(Hl[:, cc, :], oT[:, cc, :], Hh[:, cc, :].bitcast(F32), ALU.subtract).then_inc(S("ol"), 1)
            dve.wait_ge(x_upd, 24)
            for m in range(DC):
                split_lo(U_WO + m + SPLIT_AHEAD)
                residual(3, m, U_WO + m)
            dve.wait_ge(x_upd, 32)
            norm(4)
            ffn(1)
            dve.wait_ge(x_upd, 48)
            norm(5)
            for tb in range(5):
                n = P if tb < 4 else TS
                dve.wait_ge(S("f_pe"), tb + 1)
                if tb >= 2:
                    dve.wait_ge(S(f"y_out{tb % 2}"), 16 * (tb // 2))
                V.tensor_copy(stage[0:n, tb % 2, 0:512], ps[0:n, 2 * (tb % 3), :]).then_inc(S("fe_dve"), 1)

        @block.tensor
        def _(pe):
            M = nc.tensor.matmul

            def tr(out, in_):
                return nc.tensor.transpose(out, in_, ident[0:in_.shape[0], 0:in_.shape[0]])

            def dense(u, hi, lo, ready=None):
                K, w = UNITS[u][2], UNITS[u][4]
                s = u % RING
                pe.wait_ge(lo_ready, u + 1)
                if u >= RING:
                    pe.wait_ge(tile_free, u - RING + 1)
                last = None
                for k in range(K):
                    if ready:
                        ready(k)
                    for i, (wt, rt) in enumerate(((wh, hi), (wh, lo), (wl, hi))):
                        for h in range(2):
                            last = M(ps[0:w, 2 * s + h, 0:HT], wt[:, s, k, 0:w], rt[:, k, h * HT:(h + 1) * HT],
                                     start=(k == 0 and i == 0), stop=(k == K - 1 and i == 2))
                last.then_inc(tile_done, 1)

            def ada_unit(n):
                pe.wait_ge(ada_in[n % 3], 16 * (n // 3 + 1))
                if n >= 2:
                    pe.wait_ge(ada_ev, 2 * (n - 1))
                last = None
                for k in range(2):
                    for cc in range(DC):
                        last = M(ps[:, 6 + n % 2, k * 16:k * 16 + 9], ada[:, n % 3, cc, k * P:(k + 1) * P], cT[:, cc::DC],
                                 start=(cc == 0), stop=(cc == DC - 1))
                last.then_inc(ada_used, 1)

            def sum_squares(sem, base_, done):
                for cc in range(DC):
                    pe.wait_ge(sem, base_ + cc + 1)
                    for h in range(2):
                        last = M(ps[:, 6 + h, 0:HT], ones[:], sqb[:, cc, h * HT:(h + 1) * HT],
                                 start=(cc == 0), stop=(cc == DC - 1))
                last.then_inc(done, 1)

            def normed(k):
                def ready(cc):
                    pe.wait_ge(S("n_lo"), 9 * k + cc + 2)
                return ready

            pe.wait_ge(S("id_in"), 16)
            pe.wait_ge(S("vec_in"), 16 * 11)
            tr(ps[:, 7, 0:R_END], rows0[0:R_END, 0, :])
            tr(ps[:, 7, R_END:R_END + 124], rows0[0:124, 1, :])
            tr(ps[:, 7, R_END + 124:R_END + 248], rows0[0:124, 2, :])
            tr(ps[:, 7, 384:512], rows0[:, 3, :]).then_inc(S("vec_pe"), 1)
            pe.wait_ge(S("c_silu"), 1)
            tr(ps[:, 6, 0:72], rows0[0:72, 4, :]).then_inc(S("vec_pe"), 1)
            for bk in range(7):
                n = xi_rows[bk]
                pe.wait_ge(S(f"xi_in{bk % 2}"), 16 * (bk // 2 + 1))
                if bk >= 3:
                    pe.wait_ge(S("xi_dve"), bk - 2)
                    pe.wait_ge(S("xi_act"), bk - 2)
                for cc in range(DC):
                    last = tr(ps[:, 2 * (bk % 3) + cc // 4, (cc % 4) * n:(cc % 4 + 1) * n],
                              stage[0:n, bk % 2, cc * P:(cc + 1) * P])
                last.then_inc(S("xi_pe"), 1)
            pe.wait_ge(S("const"), 3)
            pe.wait_ge(S("vec_act"), 1)
            pe.wait_ge(S("vec_dve"), 3)
            sum_squares(S("st_sq"), 0, S("st_ss"))
            pe.wait_ge(S("st_rms"), 1)
            for n in range(ADA_FIRST):
                ada_unit(n)
            n_ada = ADA_FIRST
            pe.wait_ge(S("xi_dve"), 7)
            pe.wait_ge(S("xi_act"), 7)
            for u in range(U_PW2):
                dense(u, Hh, Hl, normed(0) if u == 0 else None)
                for _k in range(ADA_PW1):
                    ada_unit(n_ada)
                    n_ada += 1
            pe.wait_ge(tile_free, U_PW2)
            for cc in range(DC):
                tr(ps[0:CW - 1, cc // 4, (cc % 4) * P:(cc % 4 + 1) * P], u_p[:, cc, TP:TP + CW - 1])
            for cc in range(DC):
                last = tr(ps[0:TS, 2 + cc // 4, (cc % 4) * P:(cc % 4 + 1) * P],
                          u_s[:, cc, CW - 1:, :].rearrange("p t b -> p (t b)"))
            last.then_inc(S("cr_pe"), 1)
            while n_ada < N_ADA:
                ada_unit(n_ada)
                n_ada += 1
            pe.wait_ge(ada_ev, 2 * N_ADA)
            pe.wait_ge(S("convs"), 2 * CW)
            for cc in range(DC):
                pe.wait_ge(S("conv"), CW * (cc + 1))
                for h in range(2):
                    last = M(ps[:, 6 + h, 0:HT], ones[:], y[:, cc, h * HT:(h + 1) * HT], start=(cc == 0), stop=(cc == DC - 1))
            last.then_inc(S("ln_pe"), 1)
            pe.wait_ge(S("ln_mu"), 1)
            sum_squares(S("ln_sq"), 0, S("ln_pe"))

            def ln_ready(cc):
                pe.wait_ge(S("ln_lo"), cc + 1)

            pe.wait_ge(S("cr_ev"), 2)
            for m in range(DC):
                dense(U_PW2 + m, Hh, Hl, ln_ready if m == 0 else None)

            def ffn(layer, k):
                for hf in range(2):
                    u0 = U_FFN[layer] + hf * F_UNITS
                    q0 = (2 * layer + hf) * FHC
                    for p in range(2 * FHC):
                        dense(u0 + p, Hh, Hl, normed(k) if p == 0 and hf == 0 else None)

                    def ready(cc):
                        pe.wait_ge(S("ff_lo"), q0 + cc + 1)

                    for m in range(DC):
                        dense(u0 + 2 * FHC + m, ah, al, ready if m == 0 else None)

            sum_squares(S("st_sq"), 8, S("st_ss"))
            ffn(0, 1)
            sum_squares(S("st_sq"), 16, S("st_ss"))
            for f in range(12):
                dense(U_KV + f, Hh, Hl, normed(2) if f == 0 else None)
            pe.wait_ge(tile_free, U_IN)
            pe.wait_ge(S("st_rms"), 3)
            for tb in range(5):
                n = P if tb < 4 else TS
                for g3 in range(3):
                    k = 3 * tb + g3
                    if k >= 2:
                        done = 5 * ((k - 2) // 3) + (1, 3, 5)[(k - 2) % 3]
                        pe.wait_ge(S("rt_ev"), done)
                    for ff in range(4):
                        last = tr(ps[0:n, 6 + k % 2, ff * P:(ff + 1) * P],
                                  kvT[:, KV_SLOT[4 * g3 + ff], tb * P:tb * P + n])
                    last.then_inc(S("rt_pe"), 1)
            for t in range(DC + 1):
                dense(U_IN + t, Hh, Hl, normed(3) if t == 0 else None)
            pe.wait_ge(S("q_act"), 2 * DC + 1)
            pe.wait_ge(S("rt_ev"), 25)
            for i in range(4):
                last = tr(ps[:, 6, 48 * i:48 * i + 48], t2[0:3 * NH, 0, P * i:P * i + P])
            last.then_inc(S("gs_pe"), 1)
            pe.wait_ge(S("cb_in"), 16 * 7)
            for br in range(3):
                last = M(ps[:, 7, TS * br:TS * br + TS], expd[:, br, :], t2[0:3 * NH, 0, TP:T], start=True, stop=True)
            last.then_inc(S("gs_pe"), 1)
            pe.wait_ge(S("w1_in"), 32)
            pe.wait_ge(S("gates"), 1)
            w1s = (w1k, w1v)
            for t in range(2):
                for j in range(LC // 2):
                    last = M(ps[:, 6, t:t + 1], w1s[t][:, j, :], vT[:, R_PE + 16 * t + j:R_PE + 16 * t + j + 1],
                             start=(j == 0), stop=(j == LC // 2 - 1))
            last.then_inc(S("hp_pe"), 1)
            pe.wait_ge(S("p2"), 16)
            pe.wait_ge(tile_free, U_WO)
            for t in range(2):
                for j in range(LC // 2):
                    last = M(ps[:, t, 0:G * NCP], w1s[t][:, j, :],
                             P2[:, NKV * t:NKV * t + NKV, j:j + 8 * (NCP - 1) + 1:8],
                             start=(j == 0), stop=(j == LC // 2 - 1))
                last.then_inc(S("hp_pe"), 1)
            pe.wait_ge(S("hc"), 3)
            M(ps[0:HD, 2, 0:G * NCP], w2t[:, 0, :], t2[:, 0, 0:G * NCP], start=True, stop=True).then_inc(S("kc_pe"), 1)
            for h in range(NKV):
                last = M(ps[0:NCP, 3, h * HD:(h + 1) * HD], t2[:, 0, P + h * NCP:P + (h + 1) * NCP], w2t[:, 1, :],
                         start=True, stop=True)
            last.then_inc(S("kc_pe"), 1)
            for g2 in range(2):
                for bb in range(4):
                    b = 4 * g2 + bb
                    pe.wait_ge(S(f"cc_in{b % 2}"), 64 * (b // 2 + 1))
                    if b:
                        pe.wait_ge(S("cp_dve"), b)
                        pe.wait_ge(S("cp_act"), b)
                    for t in range(2):
                        for h in range(NKV):
                            last = tr(ps[:, 4 + t, h * P:(h + 1) * P],
                                      Cb[b % 2][:, NKV * t + h].rearrange("p e d -> p (e d)"))
                    last.then_inc(S("ct_pe"), 1)
                pe.wait_ge(S("cp_dve"), 4 * g2 + 4)
                pe.wait_ge(S("cp_act"), 4 * g2 + 4)
                if g2:
                    pe.wait_ge(S("hc"), 5)
                n = 4 * NKV * NCS
                for t, cp in enumerate((CPk, CPv)):
                    for j in range(LC // 2):
                        last = M(ps[:, t, 0:n], w1s[t][:, j, :],
                                 cp[:].rearrange("p b h q -> p (b h) q")[:, :, j:j + 8 * (NCS - 1) + 1:8],
                                 start=(j == 0), stop=(j == LC // 2 - 1))
                    last.then_inc(S("hs_pe"), 1)
                pe.wait_ge(S("hc"), 4 + 2 * g2)
                pe.wait_ge(S("kc_dve"), 3 if g2 == 0 else 5)
                M(ps[0:HD, 2, 0:n], w2t[:, 0, :], t2[:, 1, 0:n], start=True, stop=True).then_inc(S("kc_pe"), 1)
            pe.wait_ge(S("kc_dve"), 7)
            pe.wait_ge(S("hc"), 7)

            def scores(n):
                kv, i = n // 4, n % 4
                L, b64 = P * (i + 1), 64 * (kv % 2)

                def free(k):
                    if k >= 4:
                        pe.wait_ge(S("sc"), k - 3)

                for s in range(8):
                    k = 9 * n + s
                    free(k)
                    M(ps[:, k % 4, 0:L], qT[b64:b64 + 64, (kv // 2) * 4 + s // 2, P * i:P * i + P],
                      kvT[b64:b64 + 64, 2 * (s % 2) + kv // 2, 0:L], start=True, stop=True).then_inc(S("sc_pe"), 1)
                k = 9 * n + 8
                free(k)
                for g in range(G):
                    last = M(ps[:, k % 4, g * NCP:(g + 1) * NCP], qT[b64:b64 + 64, (kv // 2) * 4 + g, P * i:P * i + P],
                             kcT_p[b64:b64 + 64, kv // 2, :], start=True, stop=True)
                last.then_inc(S("sc_pe"), 1)

            def values(n):
                kv, i = n // 4, n % 4
                steps = [(br, kb) for br in range(2) for kb in range(i + 1)] + [(2, 0)]
                pe.wait_ge(S("scaled"), 8 * (n + 1))
                pe.wait_ge(S("wg"), 4 * (n + 1))
                if n >= 2:
                    pe.wait_ge(S("o_act") if n % 2 else S("o_dve"), 2 * (n // 2))

                def turn(x_):
                    j, (br, kb) = pt0[n] + x_, steps[x_]
                    if j >= 2:
                        pe.wait_ge(S("pt_act") if j % 2 else S("pt_dve"), j // 2)
                    for g in range(G):
                        src = Pp[:, n % 2, 2 * g + br, kb * P:(kb + 1) * P] if br < 2 else Pc[:, n % 2, g, :]
                        K = P if br < 2 else NCP
                        last = tr(ps[0:K, 4 + j % 2, g * P:(g + 1) * P], src)
                    last.then_inc(S("pt_pe"), 1)

                def product(x_):
                    j, (br, kb) = pt0[n] + x_, steps[x_]
                    pe.wait_ge(S("pt_act") if j % 2 else S("pt_dve"), j // 2 + 1)
                    v = vrow[:, kb, br, kv, :] if br < 2 else vc_p[0:NCP, kv, :]
                    K = P if br < 2 else NCP
                    M(ps[0:HD, 6 + n % 2, :], v, PT[0:K, j % 2, :], start=(x_ == 0), stop=(x_ == len(steps) - 1))\
                        .then_inc(S("pv"), 1)

                for x_ in range(len(steps)):
                    turn(x_)
                    if x_:
                        product(x_ - 1)
                product(len(steps) - 1)

            for n in range(4 * NKV + 1):
                if n < 4 * NKV:
                    scores(n)
                if n:
                    values(n - 1)

            pe.wait_ge(S("sc"), 9 * 4 * NKV)
            for b in range(NB):
                for h in range(NKV):
                    q = NCS * (NKV * b + h)
                    last = M(ps[0:NCS, b // 2, (b % 2) * 256 + HD * h:(b % 2) * 256 + HD * h + HD],
                             hv_s[:, q:q + NCS], w2t[:, 1, :], start=True, stop=True)
            last.then_inc(S("vc_pe"), 1)
            pe.wait_ge(S("pt_dve"), pt0[-1] - pt0[-1] // 2)
            pe.wait_ge(S("pt_act"), pt0[-1] // 2)
            pe.wait_ge(S("vc_dve"), 1)
            pe.wait_ge(S("o_dve"), 16)
            pe.wait_ge(S("o_act"), 16)
            for b in range(NB + 1):
                if b < NB:
                    pe.wait_ge(S(f"s_in{b % 2}"), 48 * (b // 2 + 1))
                    if b:
                        pe.wait_ge(S("kt_dve"), b)
                        pe.wait_ge(S("kt_act"), b)
                    for bank, rows in ((4, Cs), (5, Cw)):
                        for kp in range(2):
                            for par in range(2):
                                q = (2 * kp + par) * P
                                last = tr(ps[:, bank, q:q + P], rows[:, b % 2, par, kp * P:(kp + 1) * P])
                    last.then_inc(S("kt_pe"), 1)
                    pe.wait_ge(S("kt_dve"), b + 1)
                    pe.wait_ge(S("kt_act"), b + 1)
                    if b >= 2:
                        pe.wait_ge(S("s_z"), 5 * (b - 1))
                    bank = 2 * (b % 2)
                    for kv in range(NKV):
                        b64, o32 = 64 * (kv % 2), 32 * kv
                        q = qs[b64:b64 + 64, kv // 2, b].rearrange("p g t -> p (g t)")
                        for br in range(2):
                            M(ps[o32:o32 + 32, bank + br, 0:PAST], q, KT[b64:b64 + 64, br, kv // 2].rearrange("p e q -> p (e q)"),
                              start=True, stop=True)
                            last = M(ps[o32:o32 + 32, bank + br, PAST:NKS], q, kvT[b64:b64 + 64, 2 * br + kv // 2, TP:T],
                                     start=True, stop=True)
                        last = M(ps[o32:o32 + 32, bank, NKS:NKS + NCS], q, kcT_s[b64:b64 + 64, kv // 2, b, :],
                                 start=True, stop=True)
                    last.then_inc(S("s_sc"), 1)
                if b >= 1:
                    m = b - 1
                    pe.wait_ge(S("s_scaled"), 2 * (m + 1))
                    pe.wait_ge(S("s_pc"), m + 1)
                    if m:
                        pe.wait_ge(S("s_ptd"), 3 * m)
                        pe.wait_ge(S("s_pta"), 2 * m)
                        pe.wait_ge(S("o_dve"), 16 + 2 * m)
                    for br in range(2):
                        for kb in range(3):
                            K = P if kb < 2 else TS
                            tr(ps[0:K, 6 + br, kb * P:(kb + 1) * P], Ps[:, m % 2, br, kb * P:kb * P + K])
                    tr(ps[0:NCS, 6, 384:512], Pcs[:, m % 2, 0:NCS]).then_inc(S("s_pt"), 1)
                    pe.wait_ge(S("s_ptd"), 3 * (m + 1))
                    pe.wait_ge(S("s_pta"), 2 * (m + 1))
                    for kv in range(NKV):
                        cols = slice(32 * kv, 32 * kv + 32)
                        parts = []
                        for br, rows in ((0, Cs), (1, Cw)):
                            for par in range(2):
                                parts.append((rows[:, m % 2, par, 256 + 64 * kv:320 + 64 * kv], PTs[:, 3 * br + par, cols]))
                            parts.append((vrow[0:TS, 4, br, kv, :], PTs[0:TS, 3 * br + 2, cols]))
                        parts.append((vc_s[:, m, kv, :], PTs[0:NCS, 6, cols]))
                        for x_, (lhs, rhs) in enumerate(parts):
                            last = M(ps[0:HD, 7, 384 + 32 * kv:416 + 32 * kv], lhs, rhs, start=(x_ == 0), stop=(x_ == 6))
                    last.then_inc(S("s_pv"), 1)

            def o_ready(cc):
                pe.wait_ge(S("ol"), cc + 1)

            pe.wait_ge(S("o_dve"), 32)
            for m in range(DC):
                dense(U_WO + m, Hh, Hl, o_ready if m == 0 else None)
            sum_squares(S("st_sq"), 24, S("st_ss"))
            ffn(1, 4)
            sum_squares(S("st_sq"), 32, S("st_ss"))
            pe.wait_ge(S("n_hi"), 9 * 5 + DC)
            pe.wait_ge(S("n_s"), 18)
            for tb in range(5):
                n = P if tb < 4 else TS
                if tb >= 3:
                    pe.wait_ge(S("fe_act"), tb - 2)
                    pe.wait_ge(S("fe_dve"), tb - 2)
                for cc in range(DC):
                    last = tr(ps[0:n, 2 * (tb % 3) + cc // 4, (cc % 4) * P:(cc % 4 + 1) * P], xf[:, cc, tb * P:tb * P + n])
                last.then_inc(S("f_pe"), 1)


_OUTS = [("y_prompt", (1, 512, 1024)), ("y_sample", (8, 8, 1024)), ("kv_prompt", (4, 128, 4, 4, 64)),
         ("kv_sample", (8, 8, 4, 4, 64)), ("win_prompt", (1, 512, 2, 4, 64)), ("win_sample", (8, 264, 2, 4, 64)),
         ("conv_prompt", (1, 1, 30, 1024)), ("conv_sample", (1, 8, 30, 1024))]


def shape_constants():
    import numpy as np

    f = np.float32
    q = np.arange(P)[:, None]
    d = q + (TP - P) - np.arange(TP)[None, :]
    dist = np.where(d >= 0, d, FAR)
    i = np.arange(4)[None, :, None]
    dc = P * i + q[:, :, None] - (ST * np.arange(NCP)[None, None, :] + LC - 1)
    distc = np.where(dc >= 0, dc, FAR)
    row_h, row_t = np.arange(P) // NT, np.arange(P) % NT
    sl = np.array(SLOPES)[row_h][:, None]
    pos = np.concatenate([2 * np.arange(P), 2 * np.arange(P) + 1])
    tabs = np.zeros((P, NB, NKS))
    tabs[:, :, :PAST] = (sl * (PAST + row_t[:, None] - pos[None, :]))[:, None, :]
    dn = row_t[:, None] - np.arange(NT)[None, :]
    tabs[:, :, PAST:] = FAR
    for b in range(NB):
        tabs[:, b, PAST + NT * b:PAST + NT * b + NT] = np.where(dn >= 0, sl * dn, FAR)
    tabc = sl * (PAST + row_t[:, None] - (ST * np.arange(NCS)[None, :] + LC - 1))
    expd = np.zeros((3 * NH, 3, P))
    for h in range(NH):
        for br in range(3):
            expd[3 * h + br, br, NT * h:NT * h + NT] = 1
    return {"ident": np.eye(P).astype(f), "dist": dist.astype(f), "distc": distc.astype(f),
            "maskc": (dc[:, 0, :] >= 0).astype(f), "tmask": (row_t[:, None] == np.arange(NT)[None, :]).astype(f),
            "tabs": tabs.astype(f), "tabc": tabc.astype(f), "expd": expd.astype(f)}


def kernel(**inputs):
    import numpy as _np
    import concourse.bacc as _bacc
    from concourse import mybir as _mybir
    from concourse.bass_utils import run_bass_kernel_spmd as _run

    nc = _bacc.Bacc("TRN2", target_bir_lowering=False, num_devices=1)
    arrays, a, o, c = {}, {}, {}, {}
    for group, named in ((a, inputs), (c, shape_constants())):
        for name, v in named.items():
            v = _np.ascontiguousarray(v)
            key = f"in_{name}_dram"
            arrays[key] = v
            group[name] = nc.dram_tensor(key, v.shape, _mybir.dt.from_np(v.dtype), kind="ExternalInput").ap()
    for name, shape in _OUTS:
        o[name] = nc.dram_tensor(f"out_{name}_dram", shape, F32, kind="ExternalOutput").ap()
    build(nc, a, o, c)
    res = _run(nc, [arrays], core_ids=[0])
    return tuple(res.results[0][f"out_{name}_dram"] for name, _ in _OUTS)
```

```python
from contextlib import ExitStack

import concourse.bass as bass
from concourse import mybir

F32 = mybir.dt.float32
F32R = mybir.dt.float32r
I32 = mybir.dt.int32
ACT = mybir.ActivationFunctionType
ALU = mybir.AluOpType
AX = mybir.AxisListType

P = 128
D = 1024
DC = D // P
TP = 512
NB, NT = 8, 8
TS = NB * NT
T = TP + TS
HT = T // 2
CW = 31
FF = 2816
FH = FF // 2
FHC = FH // P
NH, NKV, G, HD = 16, 4, 4, 64
LC, ST = 32, 16
NCP = (TP - LC) // ST + 1
PAST = 256
NCS = (PAST + NT - LC) // ST + 1
PG = 128
NPG = PAST // PG
EPS = 1e-6
SCALE = HD ** -0.5
NKS = PAST + TS
FAR = 1e32
SLOPES = [2.0 ** (-8.0 * (h + 1) / NH) for h in range(NH)]

R_NG, R_B1, R_BDW, R_LNG, R_LNB, R_KVG, R_FING, R_PE, R_END = 0, 32, 48, 56, 64, 72, 80, 88, 120

NORMS = [(R_NG, 0, 1), (R_NG + 8, 3, 4), (R_KVG, 12, 13), (R_NG + 16, 6, 7), (R_NG + 24, 9, 10), (R_FING, 14, 15)]
STAT_OF = [0, 1, 2, 2, 3, 4]
GATES = [2, 5, 5, 8, 11, 11]

UNITS = []
for _j in range(DC):
    UNITS += [("pw1", 0, DC, _j * P, P), ("pw1", 0, DC, D + _j * P, P)]
U_PW2 = len(UNITS)
UNITS += [("pw2", 0, DC, _m * P, P) for _m in range(DC)]


def _ffn_units(layer):
    out = []
    for hf in range(2):
        for p in range(FHC):
            out += [(f"up{layer}", 0, DC, hf * FH + p * P, P), (f"up{layer}", 0, DC, FF + hf * FH + p * P, P)]
        out += [(f"down{layer}", hf * FH, FHC, m * P, P) for m in range(DC)]
    return out


U_FFN = [len(UNITS), 0]
UNITS += _ffn_units(0)
U_KV = len(UNITS)
UNITS += [("kv", 0, DC, _m * P, P) for _m in range(12)]
U_IN = len(UNITS)
UNITS += [("in", 0, DC, _m * P, P) for _m in range(DC)] + [("in", 0, DC, D, 3 * NH)]
U_WO = len(UNITS)
UNITS += [("wo", 0, DC, _m * P, P) for _m in range(DC)]
U_FFN[1] = len(UNITS)
UNITS += _ffn_units(1)
NU = len(UNITS)
F_UNITS = 2 * FHC + DC
SMP_CONV = [(0, 4), (4, 7)]
RING = 3
LOOP_PAIRS = 3
LOOPS = FHC // LOOP_PAIRS
assert 2 * LOOP_PAIRS % RING == 0

STRIP = 512
N_STRIP = 16 * D // STRIP
STRIPS_FIRST = 4
STRIP_BLOCKS = [1, 2, 3, 4]
STRIP_PLAN = [1, 1, 0] + [2] * 13
assert len(STRIP_PLAN) == U_PW2 and sum(STRIP_PLAN) == N_STRIP - STRIPS_FIRST
RING_ADA = 3

KV_SLOT = {4: 0, 5: 1, 8: 2, 9: 3, 0: 4, 1: 5, 2: 6, 3: 7, 6: 8, 7: 9, 10: 10, 11: 11}


def build(nc, a, o, c):
    ctx = ExitStack()
    with ctx:
        sems = {}

        def S(name):
            if name not in sems:
                sems[name] = ctx.enter_context(nc.semaphore(name))
            return sems[name]

        base = [(nc.sbuf_base + 31) // 32 * 32]

        def at(name, shape, off, dt=F32):
            return nc.alloc_sbuf_tensor_at(name, shape, dt, offset=off)

        def place(name, shape, dt=F32):
            n = 4
            for s in shape[1:]:
                n *= s
            off = base[0]
            base[0] += (n + 31) // 32 * 32
            return at(name, shape, off, dt)

        def region(nbytes):
            off = base[0]
            base[0] += (nbytes + 31) // 32 * 32
            return off

        x = place("x", [P, DC, T])
        rH = region(2 * DC * T * 4)
        Hh = at("Hh", [P, DC, T], rH, F32R)
        Hl = at("Hl", [P, DC, T], rH + DC * T * 4, F32R)
        sqb = at("sqb", [P, DC, T], rH)
        xf = at("xf", [P, DC, T], rH)
        rF = region(2 * FHC * T * 4)
        ah = at("ah", [P, FHC, T], rF, F32R)
        al = at("al", [P, FHC, T], rF + FHC * T * 4, F32R)
        u_p = at("u_p", [P, DC, CW - 1 + TP], rF)
        u_s = at("u_s", [P, DC, CW - 1 + NT, NB], rF + DC * (CW - 1 + TP) * 4)
        y = at("y", [P, DC, T], rF + (DC * (CW - 1 + TP) + DC * NB * (CW - 1 + NT)) * 4)
        assert DC * (CW - 1 + TP) + DC * NB * (CW - 1 + NT) + DC * T <= 2 * FHC * T
        rows0 = at("rows0", [P, 5, P], rF + DC * (CW - 1 + TP) * 4 + DC * NB * (CW - 1 + NT) * 4)
        kvT = at("kvT", [P, 12, T], rF)
        oT = at("oT", [P, DC, T], rF + 4 * T * 4)
        qT = at("qT", [P, DC, T], rF + 12 * T * 4)
        off = rF + 20 * T * 4
        kcT_p = at("kcT_p", [P, 2, NCP], off)
        vc_p = at("vc_p", [32, NKV, HD], off + 256)
        kcT_s = at("kcT_s", [P, 2, NB, NCS], off + 1280)
        hv_s = at("hv_s", [P, NB * NKV * NCS], off + 2240)
        assert off + 2240 + 1920 <= rF + 2 * FHC * T * 4
        raw = place("raw", [P, RING, FHC, P])
        wh = place("wh", [P, RING, FHC, P], F32R)
        wl = place("wl", [P, RING, FHC, P], F32R)
        mods = place("mods", [P, 16 * DC, 1 + NB])
        rA = region(RING_ADA * 4 * STRIP * 4)
        ada = at("ada", [P, RING_ADA, 4, STRIP], rA)
        vrow = at("vrow", [P, 5, 2, NKV, HD], rA)
        o1 = rA + 5 * 512 * 4
        bias = at("bias", [P, G, TP], o1)
        Cb = [at("C0", [P, 2 * NKV, 2, HD], rA), at("C1", [P, 2 * NKV, 2, HD], rA + 4096)]
        w1k = at("w1k", [P, LC // 2, P], rA + 8192)
        w1v = at("w1v", [P, LC // 2, P], rA + 16384)
        vc_s = at("vc_s", [NCS, NB, NKV, HD], o1)
        o2 = o1 + 8192
        PT = at("PT", [P, 2, G * P], o2)
        PTs = at("PTs", [P, 7, P], o2)
        winst = at("winst", [P, 2, 512], o2)
        o3 = o2 + 4096
        gates = at("gates", [P, 4, NH, 3], o3)
        gs = at("gs", [P, 3, NB], o3 + 768)
        nmin = at("nmin", [P, 2, 12], o3 + 896)
        sums = at("sums", [P, 2, 12], o3 + 1024)
        wgt = at("wgt", [P, 2, 12], o3 + 1152)
        assert o3 + 1312 <= rA + RING_ADA * 4 * STRIP * 4
        CPk = at("CPk", [P, 4, NKV, P], rF + 12 * T * 4)
        CPv = at("CPv", [P, 4, NKV, P], rF + 12 * T * 4 + 8192)
        expd = at("expd", [3 * NH, 3, P], rH + 34816)
        Pp = at("Pp", [P, 2, 8, TP], rH)
        Pc = at("Pc", [P, 2, G, NCP], rH + 32768)
        tabs = at("tabs", [P, NB, NKS], rH)
        Ps = at("Ps", [P, 2, 2, NKS], rH + 10240)
        Pcs = at("Pcs", [P, 2, 16], rH + 15360)
        slots = [rH + 15488, rH + 15488 + 8192, rF + 12 * T * 4, rF + 12 * T * 4 + 8192]
        Cs = [at(f"Cs{i}", [P, 2, 512], off_) for i, off_ in enumerate(slots)]
        Cw = [at(f"Cw{i}", [P, 2, 512], off_ + 4096) for i, off_ in enumerate(slots)]
        KT = at("KT", [P, 2, 2, 2, P], rH + 15488 + 16384)
        assert 15488 + 16384 + 4096 <= 2 * DC * T * 4
        t2 = place("t2", [P, 2, T])
        r = place("r", [P, T])
        rMu = region(T * 4)
        mu = at("mu", [P, T], rMu)
        dist = at("dist", [P, TP], rMu)
        adarow = at("adarow", [P, STRIP], rMu)
        rS = region(DC * TS * 4)
        fs = at("fs", [P, DC, TS], rS)
        qs = at("qs", [P, 2, NB, G, NT], rS)
        rG = region(2 * D * 4)
        stage = at("stage", [P, 2, D], rG)
        P2 = at("P2", [P, 2 * NKV, TP // 2], rG)
        ident = place("ident", [P, P])
        ones = place("ones", [P, P])
        vT = place("vT", [P, R_END])
        wdT = place("wdT", [P, CW * DC])
        rB = region(P * 4)
        badaT = at("badaT", [P, P], rB)
        w2t = at("w2t", [P, 2, HD], rB)
        cpad = place("cpad", [P, DC, 32])
        sel = place("sel", [P, 1 + NB])
        peb = place("peb", [P, 2])
        acoef = place("acoef", [P, DC, 1 + NB])
        epst = place("epst", [P, 1])
        scrap = place("scrap", [P, 1])
        distc = place("distc", [P, 4, NCP])
        maskc = place("maskc", [P, NCP])
        tmask = place("tmask", [P, NT])
        tabc = place("tabc", [P, NCS])
        rtmp = place("rtmp", [P, 2, TS])
        pgt = place("pgt", [1, NB * NPG], I32)
        assert base[0] <= nc.sbuf_usable_end, (base[0], nc.sbuf_usable_end)

        ps = ctx.enter_context(nc.psum_tensor("ps", [P, 8, 512], F32))

        def tile(u, w=P):
            s = 2 * (u % RING)
            return ps[0:w, s:s + 2, 0:HT]

        def halves(ap):
            return ap.rearrange("p (b t) -> p b t", b=2)

        def sums_done(st):
            return DC + 2 * st

        def smp_cols(t_):
            return t_[:, 1, HT - TS:HT].rearrange("p (b t) -> p b t", b=NB)

        stats = ps[:, 6:8, 0:HT]

        raw_in = [S(f"raw_in{i}") for i in range(RING)]
        hi_ready, lo_ready = S("hi_ready"), S("lo_ready")
        tile_done, tile_free = S("tile_done"), S("tile_free")
        ada_in = [S(f"ada_in{i}") for i in range(3)]
        ada_used, ada_row, ada_tr, ada_ev = S("ada_used"), S("ada_row"), S("ada_tr"), S("ada_ev")
        x_upd = S("x_upd")

        W = {"pw1": a["conv_w_pw1"][0], "pw2": a["conv_w_pw2"][0], "kv": a["w_kv"],
             "in": a["nsa_w_in"][0], "wo": a["nsa_w_o"][0],
             "up0": a["ffn_w_up"][0], "up1": a["ffn_w_up"][1],
             "down0": a["ffn_w_down"][0], "down1": a["ffn_w_down"][1]}
        wada = a["w_ada"].rearrange("(c p) n -> p c n", p=P)

        def load_unit(sp, u, shift=0):
            name, r0, K, c0, w = UNITS[u]
            slot = u % RING
            src = W[name][r0:r0 + K * P, :].rearrange("(c p) n -> p c n", p=P)
            sp.dma_start(raw[:, slot, 0:K, 0:w], src[:, :, bass.ds(c0 + shift, w)]).then_inc(raw_in[slot], 16)

        def load_ada(sp, n):
            if n >= RING_ADA:
                sp.wait_ge(ada_used, n - RING_ADA + 1)
            c0, k0 = n // 2 * STRIP, n % 2 * 4
            sp.dma_start(ada[:, n % RING_ADA], wada[:, k0:k0 + 4, c0:c0 + STRIP]).then_inc(ada_in[n % RING_ADA], 16)

        SPLIT_AHEAD = 3
        xi_rows = [P, P, P, P, TS, 120, 120]
        page_rows = a["cache_kv"].rearrange("n (q e) t h d -> n q e (t h d)", e=2)
        win_rows = a["state_win"].rearrange("b (q e) t h d -> b q e (t h d)", e=2)
        kvp = o["kv_prompt"].rearrange("n s t h d -> n s (t h d)")
        kvs = o["kv_sample"].rearrange("b s t h d -> (b s) (t h d)")
        wps = o["win_prompt"].rearrange("b (n s) t h d -> (b n) s (t h d)", s=P)
        wss = o["win_sample"].rearrange("b s t h d -> b s (t h d)")

        CMP_PLAN = {0: [], 1: [], 2: [("bias", 0), ("turn", 0), ("turn", 1)], 3: [("turn", 2), ("turn", 3)],
                    4: [("hidden", 0)], 5: [("keys", 0)], 6: [("turn", 4), ("turn", 5)], 7: [("turn", 6), ("turn", 7)],
                    8: [("hidden", 1)], 9: [("keys", 1)], 10: [("pairs", 0)], 11: [("prompt", 0), ("prompt_out", 0)]}
        RT_PLAN = {0: [], 1: [0], 2: [1, 2], 3: [3, 4], 4: [5, 6], 5: [7, 8], 6: [9, 10, 11], 7: [12, 13, 14]}

        pt0 = [0]
        for n in range(4 * NKV):
            pt0.append(pt0[-1] + 2 * (n % 4 + 1) + 1)

        block = ctx.enter_context(nc.Block())

        @block.sync
        def _(sp):
            sp.dma_start(ident[:], c["ident"]).then_inc(S("id_in"), 16)
            sp.dma_start(sel[:], c["sel"]).then_inc(S("id_in"), 16)
            vrows = rows0[0:R_END, 0, :]
            at_row = 0
            for name, n in (("norm_g", 32), ("conv_b_pw1", 16), ("conv_b_dw", 8), ("conv_ln_g", 8),
                            ("conv_ln_b", 8), ("kv_norm_g", 8), ("final_norm_g", 8), ("pe_cmp", 32)):
                flat = a[name]
                dims = "abcd"[:len(flat.shape)]
                if len(dims) > 1:
                    flat = flat.rearrange(f"{' '.join(dims)} -> ({' '.join(dims)})")
                sp.dma_start(vrows[at_row:at_row + n, :], flat.rearrange("(r p) -> r p", p=P)).then_inc(S("vec_in"), 16)
                at_row += n
            wd = a["conv_w_dw"].rearrange("a w (c p) -> (a w c) p", p=P)
            for i in range(2):
                sp.dma_start(rows0[0:124, 1 + i, :], wd[124 * i:124 * i + 124, :]).then_inc(S("vec_in"), 16)
            sp.dma_start(rows0[:, 3, :], a["b_ada"].rearrange("(r p) -> r p", p=P)).then_inc(S("vec_in"), 16)
            sp.dma_start(rows0[0:8, 4, :], a["c_prompt"].rearrange("b (k p) -> (b k) p", p=P)).then_inc(S("c_in"), 16)
            sp.dma_start(rows0[8:72, 4, :], a["c_sample"].rearrange("b (k p) -> (b k) p", p=P)).then_inc(S("c_in"), 16)
            n_ada = 0
            for u in range(RING):
                load_unit(sp, u)
            while n_ada < 2 * STRIPS_FIRST + RING_ADA:
                load_ada(sp, n_ada)
                n_ada += 1
            u_next = RING
            for u in range(U_PW2):
                sp.wait_ge(lo_ready, u_next - RING + 1)
                load_unit(sp, u_next)
                u_next += 1
                for _k in range(2 * STRIP_PLAN[u]):
                    if n_ada < 2 * N_STRIP:
                        load_ada(sp, n_ada)
                        n_ada += 1

            def plain(to):
                nonlocal u_next
                while u_next < to:
                    sp.wait_ge(lo_ready, u_next - RING + 1)
                    load_unit(sp, u_next)
                    u_next += 1

            for layer in range(2):
                if layer:
                    plain(U_WO + RING)
                    for b in range(NB):
                        if b < 2:
                            sp.wait_ge(S("pt_pe"), pt0[-1])
                        elif b < 4:
                            sp.wait_ge(S("sc_pe"), 9 * 4 * NKV)
                        else:
                            sp.wait_ge(S("s_pv"), b - 3)
                        for pg in range(NPG):
                            page = sp.value_load(pgt[0:1, b * NPG + pg:b * NPG + pg + 1], min_val=0,
                                                 max_val=a["cache_kv"].shape[0] - 1)
                            n = PG // 2
                            sp.dma_start(Cs[b % 4][pg * n:(pg + 1) * n],
                                         page_rows[bass.ds(page, 1), :, :, 512:1024].rearrange("n q e f -> (n q) e f"))\
                                .then_inc(S(f"s_in{b % 4}"), 16)
                        sp.dma_start(Cw[b % 4][:], win_rows[b]).then_inc(S(f"s_in{b % 4}"), 16)
                for hf in range(2):
                    u0 = U_FFN[layer] + hf * F_UNITS
                    plain(u0)
                    n = 2 * LOOP_PAIRS
                    with sp.Fori(0, LOOPS) as i:
                        for k in range(n):
                            sp.wait_ge(lo_ready, i * n + (u0 + k - RING + 1))
                            load_unit(sp, u0 + k, shift=i * (LOOP_PAIRS * P))
                    u_next = u0 + LOOPS * n
                    plain(u0 + F_UNITS)
            plain(NU)

        @block.gpsimd
        def _(pool):
            def load_rows(bk):
                n = xi_rows[bk]
                if bk >= 2:
                    pool.wait_ge(S("xi_pe"), bk - 1)
                if bk < 4:
                    src = a["x_prompt"][0, bk * P:(bk + 1) * P, :]
                elif bk == 4:
                    src = a["x_sample"].rearrange("b t d -> (b t) d")
                else:
                    src = a["state_conv"].rearrange("l b t d -> (l b t) d")[120 * (bk - 5):120 * (bk - 4), :]
                pool.dma_start(stage[0:n, bk % 2, :], src).then_inc(S(f"xi_in{bk % 2}"), 16)

            load_rows(0)
            load_rows(1)
            nc.gpsimd.memset(ones[:], 1.0).then_inc(S("const"), 1)
            nc.gpsimd.memset(epst[:], EPS).then_inc(S("const"), 1)
            nc.gpsimd.memset(cpad[:], 0.0).then_inc(S("const"), 1)
            nc.gpsimd.memset(u_p[:, :, 0:CW - 1], 0.0).then_inc(S("const"), 1)
            for bk in range(2, 7):
                load_rows(bk)
            pool.dma_start(pgt[:], a["page_table"].rearrange("b n -> (b n)").unsqueeze(0)).then_inc(S("pg_in"), 16)
            pool.dma_start(o["conv_sample"][0, :, 0:CW - 1 - NT, :],
                           a["state_conv"][0, :, NT:CW - 1, :]).then_inc(S("thru"), 16)
            pool.dma_start(wss[:, 0:PAST, :], a["state_win"].rearrange("b s t h d -> b s (t h d)")).then_inc(S("thru"), 16)

            ysmp = y[:, :, TP:T].rearrange("p c (b t) -> p c t b", b=NB)
            fs4 = fs[:, :, :].rearrange("p c (t b) -> p c t b", b=NB)
            pool.wait_ge(S("xi_act"), 7)
            pool.wait_ge(S("xi_dve"), 7)
            step, n = S("convs"), 0
            for c0, c1 in SMP_CONV:
                cs = slice(c0, c1)

                def bc(col):
                    return col.unsqueeze(2).unsqueeze(3).to_broadcast([P, c1 - c0, NT, NB])

                pool.wait_ge(tile_free, 2 * c1)
                nc.gpsimd.tensor_tensor(ysmp[:, cs], u_s[:, cs, 0:NT, :], bc(wdT[:, c0:c1]), ALU.mult).then_inc(step, 1)
                pool.wait_ge(step, n + 1)
                nc.gpsimd.tensor_tensor(ysmp[:, cs], ysmp[:, cs], bc(vT[:, R_BDW + c0:R_BDW + c1]), ALU.add).then_inc(step, 1)
                for k in range(1, CW):
                    nc.gpsimd.tensor_tensor(fs4[:, cs], u_s[:, cs, k:k + NT, :], bc(wdT[:, k * DC + c0:k * DC + c1]),
                                            ALU.mult).then_inc(step, 1)
                    pool.wait_ge(step, n + 2 * k + 1)
                    nc.gpsimd.tensor_tensor(ysmp[:, cs], ysmp[:, cs], fs4[:, cs], ALU.add).then_inc(step, 1)
                    pool.wait_ge(step, n + 2 * k + 2)
                n += 2 * CW

            pool.wait_ge(tile_done, U_PW2 + 1)
            pool.wait_ge(ada_ev, 16 * DC)
            pool.dma_start(w2t[:], a["w_cmp2"].rearrange("t e d -> e t d")).then_inc(S("cb_in"), 16)
            pool.dma_start(distc[:], c["distc"]).then_inc(S("cb_in"), 16)
            pool.dma_start(maskc[:], c["maskc"]).then_inc(S("cb_in"), 16)
            pool.dma_start(tmask[:], c["tmask"]).then_inc(S("cb_in"), 16)
            pool.dma_start(tabc[:], c["tabc"]).then_inc(S("cb_in"), 16)
            w1 = a["w_cmp1"].rearrange("t (j l) d e -> t (l d) j e", l=2)
            pool.dma_start(w1k[:], w1[0]).then_inc(S("w1_in"), 16)
            pool.dma_start(w1v[:], w1[1]).then_inc(S("w1_in"), 16)
            pool.wait_ge(S("pg_in"), 16)
            for b in range(NB):
                if b >= 2:
                    pool.wait_ge(S("ct_pe"), b - 1)
                for pg in range(NPG):
                    page = pool.value_load(pgt[0:1, b * NPG + pg:b * NPG + pg + 1], min_val=0,
                                           max_val=a["cache_kv"].shape[0] - 1)
                    n = PG // 2
                    for e in range(2):
                        src = page_rows[bass.ds(page, 1), :, e, 0:512]
                        pool.dma_start(Cb[b % 2][pg * n:(pg + 1) * n, :, e, :],
                                       src.rearrange("n q (h d) -> (n q) h d", d=HD)).then_inc(S(f"cc_in{b % 2}"), 16)
            pool.wait_ge(S("st_ck"), sums_done(2))
            pool.dma_start(dist[:], c["dist"]).then_inc(S("dist_in"), 16)

            for tb in range(5):
                pool.wait_ge(S("rt_ev"), 5 * tb + 3)
                if tb < 4:
                    pool.dma_start(kvp[tb], stage[:, tb % 2, :]).then_inc(S(f"kv_out{tb % 2}"), 16)
                    pool.wait_ge(S("rt_ev"), 5 * tb + 5)
                    pool.dma_start(wps[tb], winst[:, tb % 2, :]).then_inc(S(f"kv_out{tb % 2}"), 16)
                else:
                    pool.dma_start(kvs, stage[0:TS, 0, :]).then_inc(S("kv_out0"), 16)
                    pool.wait_ge(S("rt_ev"), 5 * tb + 5)
                    for b in range(NB):
                        pool.dma_start(wss[b, PAST:PAST + NT, :], winst[NT * b:NT * b + NT, 0, :]).then_inc(S("win_out"), 16)
            pool.wait_ge(tile_done, U_WO)
            pool.dma_start(expd[:], c["expd"]).then_inc(S("expd_in"), 16)
            pool.wait_ge(S("kv_out0"), 16 * 5)
            pool.wait_ge(S("kv_out1"), 16 * 4)
            pool.wait_ge(S("win_out"), 16 * NB)
            for n in range(4 * NKV):
                L = P * (n % 4 + 1)
                pool.wait_ge(S("pw"), n + 1)
                for s in (0, 2, 4, 6, 1, 3, 5, 7):
                    nc.gpsimd.tensor_tensor(Pp[:, n % 2, s, 0:L], Pp[:, n % 2, s, 0:L],
                                            wgt[:, n % 2, s:s + 1].to_broadcast([P, L]), ALU.mult).then_inc(S("scaled"), 1)
            pool.wait_ge(S("pt_pe"), pt0[-1])
            pool.dma_start(tabs[:], c["tabs"]).then_inc(S("tabs_in"), 16)

            for b in range(NB):
                pool.wait_ge(S("s_wgt"), b + 1)
                for br in range(2):
                    nc.gpsimd.tensor_tensor(Ps[:, b % 2, br, :], Ps[:, b % 2, br, :],
                                            wgt[:, b % 2, 1 + br:2 + br].to_broadcast([P, NKS]),
                                            ALU.mult).then_inc(S("s_scaled"), 1)
            for tb in range(5):
                n = P if tb < 4 else TS
                pool.wait_ge(S("fe_act"), tb + 1)
                pool.wait_ge(S("fe_dve"), tb + 1)
                dst = o["y_prompt"][0, tb * P:(tb + 1) * P, :] if tb < 4 else o["y_sample"].rearrange("b t d -> (b t) d")
                pool.dma_start(dst, stage[0:n, tb % 2, :]).then_inc(S(f"y_out{tb % 2}"), 16)
            pool.wait_ge(S("y_out0"), 48)
            pool.wait_ge(S("y_out1"), 32)
            pool.wait_ge(S("thru"), 32)

        @block.scalar
        def _(act):
            A = nc.scalar.activation

            def split_hi(u, ub=None):
                if u >= NU:
                    return
                K, w = UNITS[u][2], UNITS[u][4]
                if ub is None:
                    act.wait_ge(raw_in[u % RING], 16 * (u // RING + 1))
                    if u >= RING:
                        act.wait_ge(tile_done, u - RING + 1)
                else:
                    i, n = ub
                    act.wait_ge(raw_in[u % RING], i * (16 * n // RING) + 16 * (u // RING + 1))
                    act.wait_ge(tile_done, i * n + (u - RING + 1))
                A(wh[:, u % RING, 0:K, 0:w], raw[:, u % RING, 0:K, 0:w], ACT.Copy).then_inc(hi_ready, 1)

            def strip_out(s_, turned):
                if s_ is not None:
                    act.wait_ge(ada_used, 2 * s_ + 2)
                    if s_:
                        act.wait_ge(ada_tr, s_)
                    A(adarow[:], ps[:, 6, :], ACT.Copy).then_inc(ada_row, 1)
                if turned is not None:
                    act.wait_ge(ada_tr, turned + 1)
                    for k in range(4):
                        q = 4 * turned + k
                        A(mods[:, q, :], ps[:, 7, 16 * k:16 * k + 9], ACT.Identity, bias=badaT[:, q:q + 1]).then_inc(ada_ev, 1)

            def root(st):
                act.wait_ge(S("st_tb"), st)
                A(scrap[:], epst[:], ACT.Sqrt).then_inc(S("st_tb"), 1)
                act.wait_ge(S("st_ck"), sums_done(st))
                A(halves(r[:]), stats, ACT.Sqrt, scale=1.0 / D, bias=epst[:]).then_inc(S("st_rms"), 1)

            def square(st, m):
                act.wait_ge(x_upd, DC * {1: 0, 2: 2, 3: 3, 4: 5}[st] + m + 1)
                if m >= 2:
                    act.wait_ge(S("st_add"), 6 * (st - 1) + max(m - 2, 1))
                A(t2[:, m % 2, :], x[:, m, :], ACT.Square).then_inc(S("st_sq"), 1)

            def norm_hi(k):
                sh = NORMS[k][1]
                if k == 3:
                    act.wait_ge(tile_done, U_IN)
                if k < 5:
                    act.wait_ge(S("n_s"), 3 * k + 3)
                    A(Hh[:, :, TP:T], fs[:], ACT.Copy).then_inc(S("n_hi"), 1)
                for cc in range(DC):
                    act.wait_ge(S("n_t"), DC * k + cc + 1)
                    dst = Hh if k < 5 else xf
                    A(dst[:, cc, 0:TP], t2[:, cc % 2, 0:TP], ACT.Identity,
                      bias=mods[:, sh * DC + cc, 0:1]).then_inc(S("n_hi"), 1)

            act.wait_ge(S("c_in"), 32)
            A(rows0[0:72, 4, :], rows0[0:72, 4, :], ACT.Silu).then_inc(S("c_silu"), 1)
            for u in range(SPLIT_AHEAD):
                split_hi(u)
            act.wait_ge(S("vec_pe"), 2)
            act.wait_ge(S("const"), 4)
            A(cpad[:, :, 0:1 + NB], ps[:, 6, 0:72].rearrange("p (b k) -> p k b", k=DC), ACT.Copy).then_inc(S("vec_act"), 1)

            def block_out(bk):
                act.wait_ge(S("xi_pe"), bk + 1)
                n = xi_rows[bk]
                src = ps[:, 2 * (bk % 3) + 1, 0:4 * n].rearrange("p (c t) -> p c t", c=4)
                if bk < 5:
                    dst = x[:, 4:8, bk * P:bk * P + n]
                else:
                    dst = u_s[:, 4:8, 0:CW - 1, 4 * (bk - 5):4 * (bk - 4)].rearrange("p c t b -> p c b t")
                    src = src.rearrange("p c (b t) -> p c b t", b=4)
                A(dst, src, ACT.Copy).then_inc(S("xi_act"), 1)

            for bk in range(5):
                block_out(bk)
                if bk in STRIP_BLOCKS:
                    if bk == STRIP_BLOCKS[0]:
                        act.wait_ge(S("vec_dve"), 3)
                    s_ = STRIP_BLOCKS.index(bk)
                    strip_out(s_, s_ - 1 if s_ else None)
            strip_out(None, STRIPS_FIRST - 1)
            act.wait_ge(S("xi_dve"), 5)
            act.wait_ge(S("xi_act"), 5)
            for cc in range(DC):
                A(sqb[:, cc, :], x[:, cc, :], ACT.Square).then_inc(S("st_sq"), 1)
            block_out(5)
            block_out(6)
            root(0)
            norm_hi(0)

            s_ = STRIPS_FIRST
            for j in range(DC):
                for k in range(2):
                    u = 2 * j + k
                    if STRIP_PLAN[u] > 1:
                        strip_out(s_, s_ - 1)
                        s_ += 1
                    if k == 1:
                        act.wait_ge(tile_done, u + 1)
                        if j >= 2:
                            act.wait_ge(tile_free, 2 * (j - 1))
                        else:
                            act.wait_ge(S("n_lo"), 9)
                        A(halves(t2[:, j % 2, :]), tile(u), ACT.Sigmoid,
                          bias=vT[:, R_B1 + DC + j:R_B1 + DC + j + 1]).then_inc(S("sig"), 1)
                    split_hi(u + SPLIT_AHEAD)
                    if STRIP_PLAN[u]:
                        strip_out(s_, s_ - 1 if s_ > STRIPS_FIRST else None)
                        s_ += 1
            strip_out(None, N_STRIP - 1)
            act.wait_ge(S("cr_pe"), 1)
            A(stage[0:CW - 1, 0, :].rearrange("p (b f) -> p b f", b=2), ps[0:CW - 1, 0:2, :], ACT.Copy).then_inc(S("cr_ev"), 1)
            A(stage[0:TS, 1, :].rearrange("p (b f) -> p b f", b=2), ps[0:TS, 2:4, :], ACT.Copy).then_inc(S("cr_ev"), 1)
            act.wait_ge(S("cr_ev"), 2)
            act.dma_start(o["conv_prompt"][0, 0], stage[0:CW - 1, 0, :]).then_inc(S("cr_out"), 16)
            for t in range(NT):
                act.dma_start(o["conv_sample"][0, :, CW - 1 - NT + t, :], stage[NB * t:NB * t + NB, 1, :]).then_inc(S("cr_out"), 16)

            act.wait_ge(S("ln_pe"), DC)
            A(halves(mu[:]), stats, ACT.Copy, scale=1.0 / D).then_inc(S("ln_mu"), 1)
            for cc in range(DC):
                act.wait_ge(S("ln_yc"), cc + 1)
                A(sqb[:, cc, :], y[:, cc, :], ACT.Square).then_inc(S("ln_sq"), 1)
            act.wait_ge(S("ln_pe"), 2 * DC)
            A(halves(r[:]), stats, ACT.Sqrt, scale=1.0 / D, bias=epst[:]).then_inc(S("ln_rms"), 1)
            for cc in range(DC):
                act.wait_ge(S("ln_t"), cc + 1)
                A(y[:, cc, :], t2[:, cc % 2, :], ACT.Silu, scale=vT[:, R_LNG + cc:R_LNG + cc + 1],
                  bias=vT[:, R_LNB + cc:R_LNB + cc + 1]).then_inc(S("ln_s"), 1)
                act.wait_ge(S("ln_s"), cc + 1)
                A(Hh[:, cc, :], y[:, cc, :], ACT.Copy).then_inc(S("ln_hi"), 1)
            for m in range(DC):
                split_hi(U_PW2 + m + SPLIT_AHEAD)
                square(1, m)

            def ffn(layer):
                act.wait_ge(S("n_lo"), 9 * (2 if layer == 0 else 5))
                for hf in range(2):
                    u0 = U_FFN[layer] + hf * F_UNITS
                    q0 = (2 * layer + hf) * FHC

                    for p in range(FHC):
                        ua, q = u0 + 2 * p, q0 + p
                        t = t2[:, q % 2, :]
                        act.wait_ge(tile_done, ua + 1)
                        split_hi(ua + SPLIT_AHEAD)
                        if q >= 2:
                            act.wait_ge(S("ff_lo"), q - 1)
                        A(halves(t), tile(ua), ACT.Silu).then_inc(S("ff_silu"), 1)
                        split_hi(ua + 1 + SPLIT_AHEAD)
                        act.wait_ge(tile_free, ua + 2)
                        A(ah[:, p, :], t, ACT.Copy).then_inc(S("ff_hi"), 1)
                    for m in range(DC):
                        split_hi(u0 + 2 * FHC + m + SPLIT_AHEAD)
                        if hf:
                            square(2 + 2 * layer, m)

            root(1)
            norm_hi(1)
            ffn(0)
            root(2)
            norm_hi(2)

            def cmp_turn(b):
                act.wait_ge(S("ct_pe"), b + 1)
                if b == 4:
                    act.wait_ge(S("hs_pe"), 2)
                A(CPv[:, b % 4].rearrange("p h q -> p (h q)"), ps[:, 7, :], ACT.Copy).then_inc(S("cp_act"), 1)

            def cmp_hidden(g2):
                n = 4 * NKV * NCS
                for t in range(2):
                    act.wait_ge(S("hs_pe"), 2 * g2 + t + 1)
                    if t == 0 and g2 == 1:
                        act.wait_ge(S("kc_pe"), 1)
                    dst = t2[:, 1, 0:n] if t == 0 else hv_s[:, g2 * n:(g2 + 1) * n]
                    A(dst, ps[:, 6 + t, 0:n], ACT.Silu, bias=peb[:, t:t + 1]).then_inc(S("hc"), 1)

            def cmp_bias():
                act.wait_ge(S("hp_pe"), 1)
                A(peb[:], ps[:, 6, 0:2], ACT.Copy).then_inc(S("hc"), 1)
                act.wait_ge(S("hc"), 1)

            def cmp_prompt():
                for t in range(2):
                    act.wait_ge(S("hp_pe"), 2 + t)
                    A(t2[:, 0, P * t:P * t + G * NCP], ps[:, 6 + t, 0:G * NCP], ACT.Silu, bias=peb[:, t:t + 1]).then_inc(S("hc"), 1)

            for f in range(12):
                split_hi(U_KV + f + SPLIT_AHEAD)
                if f == 3:
                    act.wait_ge(S("n_lo"), 27)
                for what, arg in CMP_PLAN[f]:
                    if what == "bias":
                        cmp_bias()
                    elif what == "turn":
                        cmp_turn(arg)
                    elif what == "hidden":
                        cmp_hidden(arg)
                    elif what == "prompt":
                        cmp_prompt()
            def rows_out(k):
                tb, g3 = k // 3, k % 3
                n = P if tb < 4 else TS
                act.wait_ge(S("rt_pe"), k + 1)
                src = ps[0:n, 6 + k % 2, :]
                if g3 == 0 and tb >= 2:
                    act.wait_ge(S(f"kv_out{tb % 2}"), 32 * (tb // 2))
                if g3 == 0 and tb == 0:
                    act.wait_ge(S("cr_out"), 16 * (1 + NT))
                dst = stage[0:n, tb % 2, 512 * g3:512 * g3 + 512] if g3 < 2 else winst[0:n, tb % 2, :]
                A(dst, src, ACT.Copy).then_inc(S("rt_ev"), 1)
                if g3:
                    A(vrow[0:n, tb, g3 - 1].rearrange("p h d -> p (h d)"), src[:, 256:512], ACT.Copy).then_inc(S("rt_ev"), 1)

            norm_hi(3)
            for t in range(DC):
                u = U_IN + t
                split_hi(u + SPLIT_AHEAD)
                act.wait_ge(tile_done, u + 1)
                kv = t // 2
                A(halves(qT[64 * (kv % 2):64 * (kv % 2) + 64, (kv // 2) * 4 + 2 * (t % 2), :]), tile(u)[0:64],
                  ACT.Copy, scale=-SCALE).then_inc(S("q_act"), 1)
                A(qs[64 * (kv % 2):64 * (kv % 2) + 64, kv // 2, :, 2 * (t % 2), :], smp_cols(tile(u)[0:64]),
                  ACT.Copy, scale=-SCALE).then_inc(S("q_act"), 1)
                for k in RT_PLAN[t]:
                    rows_out(k)
            u = U_IN + DC
            split_hi(u + SPLIT_AHEAD)
            act.wait_ge(tile_free, u + 1)
            A(t2[0:3 * NH, 0, :], t2[0:3 * NH, 0, :], ACT.Sigmoid).then_inc(S("q_act"), 1)

            def exps(n):
                L = P * (n % 4 + 1)
                for s in range(8):
                    act.wait_ge(S("sc"), 9 * n + s + 1)
                    A(Pp[:, n % 2, s, 0:L], Pp[:, n % 2, s, 0:L], ACT.Exp, scale=-1.0, bias=nmin[:, n % 2, s:s + 1],
                      accum_out=sums[:, n % 2, s:s + 1]).then_inc(S("pexp"), 1)

            def odd_block(m, j):
                act.wait_ge(S("pt_pe"), j + 1)
                act.wait_ge(S("pv"), j - 1)
                K = NCP if j == pt0[m] else P
                A(PT[0:K, 1, :], ps[0:K, 5, :], ACT.Copy).then_inc(S("pt_act"), 1)

            for n in range(4 * NKV + 1):
                if n < 4 * NKV:
                    exps(n)
                if n == 0:
                    act.wait_ge(S("gs_pe"), 1)
                    A(gates[:].rearrange("p i h r -> p i (h r)"),
                      ps[:, 6, 0:4 * 48].rearrange("p (i f) -> p i f", i=4), ACT.Copy).then_inc(S("gates"), 1)
                m = n - 1
                odd = range(pt0[m] + 1 - pt0[m] % 2, pt0[n], 2) if n else []
                for j in odd[:1]:
                    odd_block(m, j)
                if n < 4 * NKV:
                    act.wait_ge(S("zc"), 2 * n + 2)
                    A(Pc[:, n % 2], Pc[:, n % 2], ACT.Exp, scale=-1.0).then_inc(S("pexp"), 1)
                if n >= 1:
                    for j in odd[1:]:
                        odd_block(m, j)
                    if m % 2:
                        act.wait_ge(S("pv"), pt0[m + 1])
                        kv, i = m // 4, m % 4
                        A(oT[:, 2 * kv:2 * kv + 2, P * i:P * i + P],
                          ps[:, 7, 0:2 * P].rearrange("p (g q) -> p g q", g=2), ACT.Copy).then_inc(S("o_act"), 1)

            for b in range(NB + 1):
                if b < NB:
                    act.wait_ge(S("kt_pe"), b + 1)
                    if b >= 1:
                        act.wait_ge(S("s_sc"), b)
                    A(KT[:, 1], ps[:, 5, :].rearrange("p (a e q) -> p a e q", a=2, e=2), ACT.Copy).then_inc(S("kt_act"), 1)
                if b >= 1:
                    m = b - 1
                    act.wait_ge(S("s_pt"), m + 1)
                    if m:
                        act.wait_ge(S("s_pv"), m)
                    A(PTs[:, 3:5].rearrange("p a q -> p (a q)"), ps[:, 7, 0:256], ACT.Copy).then_inc(S("s_pta"), 1)
                    A(PTs[0:TS, 5], ps[0:TS, 7, 256:384], ACT.Copy).then_inc(S("s_pta"), 1)
                if b < NB:
                    for br in range(2):
                        act.wait_ge(S("s_z"), 5 * b + br + 1)
                        A(Ps[:, b % 2, br, :], Ps[:, b % 2, br, :], ACT.Exp, scale=-1.0, bias=nmin[:, b % 2, 1 + br:2 + br],
                          accum_out=sums[:, b % 2, 1 + br:2 + br]).then_inc(S("s_exp"), 1)
                    act.wait_ge(S("s_z"), 5 * b + 4)
                    A(Pcs[:, b % 2, 0:NCS], Pcs[:, b % 2, 0:NCS], ACT.Exp, scale=-1.0, bias=nmin[:, b % 2, 0:1],
                      accum_out=sums[:, b % 2, 0:1]).then_inc(S("s_exp"), 1)
            act.wait_ge(S("o_dve"), 8 + 4 * NB)
            act.wait_ge(S("s_pv"), NB)
            for cc in range(DC):
                A(Hh[:, cc, :], oT[:, cc, :], ACT.Copy).then_inc(S("oh"), 1)
            for m in range(DC):
                split_hi(U_WO + m + SPLIT_AHEAD)
                square(3, m)
            root(3)
            norm_hi(4)
            ffn(1)
            root(4)
            norm_hi(5)
            for tb in range(5):
                n = P if tb < 4 else TS
                act.wait_ge(S("f_pe"), tb + 1)
                if tb >= 2:
                    act.wait_ge(S(f"y_out{tb % 2}"), 16 * (tb // 2))
                A(stage[0:n, tb % 2, 512:1024], ps[0:n, 2 * (tb % 3) + 1, :], ACT.Copy).then_inc(S("fe_act"), 1)

        @block.vector
        def _(dve):
            V = nc.vector

            def split_lo(u):
                if u >= NU:
                    return
                K, w = UNITS[u][2], UNITS[u][4]
                dve.wait_ge(hi_ready, u + 1)
                V.tensor_tensor(wl[:, u % RING, 0:K, 0:w], raw[:, u % RING, 0:K, 0:w],
                                wh[:, u % RING, 0:K, 0:w].bitcast(F32), ALU.subtract).then_inc(lo_ready, 1)

            def norm(k):
                g0, sh, sc = NORMS[k]
                dve.wait_ge(ada_ev, 2 * max(4 * (sh + 1), 4 * (sc + 1)))
                V.scalar_tensor_tensor(acoef[:], mods[:, sc * DC:(sc + 1) * DC, :], 1.0,
                                       vT[:, g0:g0 + DC].unsqueeze(2).to_broadcast([P, DC, 1 + NB]),
                                       ALU.add, ALU.mult).then_inc(S("n_a"), 1)
                dve.wait_ge(S("n_a"), k + 1)
                f4 = fs[:].rearrange("p c (b t) -> p c b t", b=NB)
                if k == 5:
                    f4 = xf[:, :, TP:T].rearrange("p c (b t) -> p c b t", b=NB)
                f3 = fs[:] if k < 5 else xf[:, :, TP:T]

                def per_seq(ap):
                    return ap.unsqueeze(3).to_broadcast([P, DC, NB, NT])

                if k >= 1:
                    dve.wait_ge(S("convs"), 2 * CW * len(SMP_CONV))
                V.tensor_tensor(f4, x[:, :, TP:T].rearrange("p c (b t) -> p c b t", b=NB), per_seq(acoef[:, :, 1:]),
                                ALU.mult).then_inc(S("n_s"), 1)
                if k != 3:
                    dve.wait_ge(S("st_rms"), STAT_OF[k] + 1)
                    V.reciprocal(r[:], r[:]).then_inc(S("st_r"), 1)
                    dve.wait_ge(S("st_r"), STAT_OF[k] + 1)
                dve.wait_ge(S("n_s"), 3 * k + 1)
                V.tensor_tensor(f3, f3, r[:, TP:T].unsqueeze(1).to_broadcast([P, DC, TS]), ALU.mult).then_inc(S("n_s"), 1)
                dve.wait_ge(S("n_s"), 3 * k + 2)
                V.tensor_tensor(f4, f4, per_seq(mods[:, sh * DC:(sh + 1) * DC, 1:]), ALU.add).then_inc(S("n_s"), 1)

                def scaled(cc):
                    if cc >= 2:
                        dve.wait_ge(*((S("n_hi"), 9 * 5 + cc - 1) if k == 5 else (S("n_lo"), 9 * k + cc)))
                    V.scalar_tensor_tensor(t2[:, cc % 2, 0:TP], x[:, cc, 0:TP], acoef[:, cc, 0:1], r[:, 0:TP],
                                           ALU.mult, ALU.mult).then_inc(S("n_t"), 1)

                def low(cc):
                    dve.wait_ge(S("n_hi"), 9 * k + cc + 2)
                    V.scalar_tensor_tensor(Hl[:, cc, 0:TP], t2[:, cc % 2, 0:TP], mods[:, sh * DC + cc, 0:1],
                                           Hh[:, cc, 0:TP].bitcast(F32), ALU.add, ALU.subtract).then_inc(S("n_lo"), 1)

                scaled(0)
                scaled(1)
                if k < 5:
                    dve.wait_ge(S("n_hi"), 9 * k + 1)
                    V.tensor_tensor(Hl[:, :, TP:T], fs[:], Hh[:, :, TP:T].bitcast(F32), ALU.subtract).then_inc(S("n_lo"), 1)
                for cc in range(DC):
                    if k < 5:
                        low(cc)
                    if cc + 2 < DC:
                        scaled(cc + 2)

            def add_square(st, m):
                if m in (0, DC - 1):
                    return
                dve.wait_ge(S("st_sq"), DC * st + m + 1)
                if m > 1:
                    dve.wait_ge(S("st_add"), 6 * (st - 1) + m - 1)
                V.tensor_tensor(mu[:], t2[:, 0, :] if m == 1 else mu[:], t2[:, m % 2, :], ALU.add).then_inc(S("st_add"), 1)

            def residual(rs, m, u):
                g = GATES[rs] * DC + m
                t = tile(u)
                dve.wait_ge(tile_done, u + 1)
                dve.wait_ge(x_upd, DC * rs + max(m - 1, 0))
                V.tensor_tensor(rtmp[:, m % 2, :].rearrange("p (b t) -> p b t", b=NB),
                                t[:, 1, HT - TS:HT].rearrange("p (b t) -> p b t", b=NB),
                                mods[:, g, 1:].unsqueeze(2).to_broadcast([P, NB, NT]), ALU.mult).then_inc(S("r_s"), 1)
                V.scalar_tensor_tensor(x[:, m, 0:HT], t[:, 0, :], mods[:, g, 0:1], x[:, m, 0:HT],
                                       ALU.mult, ALU.add).then_inc(S("r_p"), 1)
                V.scalar_tensor_tensor(x[:, m, HT:TP], t[:, 1, 0:TP - HT], mods[:, g, 0:1], x[:, m, HT:TP],
                                       ALU.mult, ALU.add).then_inc(tile_free, 1)
                dve.wait_ge(S("r_s"), DC * rs + m + 1)
                V.tensor_tensor(x[:, m, TP:T], x[:, m, TP:T], rtmp[:, m % 2, :], ALU.add).then_inc(x_upd, 1)

            dve.wait_ge(S("vec_pe"), 1)
            V.tensor_copy(vT[:], ps[:, 7, 0:R_END]).then_inc(S("vec_dve"), 1)
            V.tensor_copy(wdT[:], ps[:, 7, R_END:R_END + 248]).then_inc(S("vec_dve"), 1)
            V.tensor_copy(badaT[:], ps[:, 7, 384:512]).then_inc(S("vec_dve"), 1)
            for u in range(SPLIT_AHEAD):
                split_lo(u)
            for bk in range(7):
                dve.wait_ge(S("xi_pe"), bk + 1)
                n = xi_rows[bk]
                src = ps[:, 2 * (bk % 3), 0:4 * n].rearrange("p (c t) -> p c t", c=4)
                if bk < 5:
                    dst = x[:, 0:4, bk * P:bk * P + n]
                else:
                    dst = u_s[:, 0:4, 0:CW - 1, 4 * (bk - 5):4 * (bk - 4)].rearrange("p c t b -> p c b t")
                    src = src.rearrange("p c (b t) -> p c b t", b=4)
                V.tensor_copy(dst, src).then_inc(S("xi_dve"), 1)
            dve.wait_ge(S("vec_dve"), 3)
            dve.wait_ge(S("xi_act"), 5)
            dve.wait_ge(S("xi_dve"), 5)
            norm(0)

            dve.wait_ge(S("const"), 4)
            taps = S("conv")
            odd_sum = r[:, 0:TP]
            taps_s, acc_s = S("conv_s"), y[:, DC - 1, TP:T].rearrange("p (b t) -> p t b", b=NB)
            for j in range(DC):
                ua = 2 * j
                split_lo(ua + SPLIT_AHEAD)
                dve.wait_ge(S("sig"), j + 1)
                ta, sg, b1 = tile(ua), t2[:, j % 2, :], vT[:, R_B1 + j:R_B1 + j + 1]
                n0 = CW - 1
                V.scalar_tensor_tensor(u_p[:, j, n0:n0 + HT], ta[:, 0, :], b1, sg[:, 0:HT], ALU.add, ALU.mult).then_inc(S("glu_p"), 1)
                V.scalar_tensor_tensor(u_p[:, j, n0 + HT:n0 + TP], ta[:, 1, 0:TP - HT], b1, sg[:, HT:TP],
                                       ALU.add, ALU.mult).then_inc(S("glu_p"), 1)
                V.scalar_tensor_tensor(u_s[:, j, n0:, :].rearrange("p t b -> p b t"), ta[:, 1, TP - HT:HT].rearrange("p (b t) -> p b t", b=NB), b1,
                                       sg[:, TP:T].rearrange("p (b t) -> p b t", b=NB), ALU.add, ALU.mult).then_inc(tile_free, 2)
                split_lo(ua + 1 + SPLIT_AHEAD)
                dve.wait_ge(S("glu_p"), 2 * (j + 1))
                n0 = (CW + 1) * j
                last = j == DC - 1
                acc, wj = [y[:, j, 0:TP], odd_sum], [wdT[:, k * DC + j:k * DC + j + 1] for k in range(3)]
                V.tensor_scalar(acc[0], u_p[:, j, 0:TP], wj[0], vT[:, R_BDW + j:R_BDW + j + 1],
                                ALU.mult, ALU.add).then_inc(taps, 1)
                if last:
                    dve.wait_ge(tile_free, 2 * DC)
                    V.tensor_scalar(acc_s, u_s[:, j, 0:NT, :], wj[0], vT[:, R_BDW + j:R_BDW + j + 1],
                                    ALU.mult, ALU.add).then_inc(taps_s, 1)
                if j == 0:
                    dve.wait_ge(S("n_lo"), 9)
                else:
                    dve.wait_ge(taps, n0)
                V.tensor_scalar(acc[1], u_p[:, j, 1:1 + TP], wj[1], None, ALU.mult).then_inc(taps, 1)
                if last:
                    dve.wait_ge(taps_s, 1)
                    V.scalar_tensor_tensor(acc_s, u_s[:, j, 1:1 + NT, :], wj[1], acc_s, ALU.mult, ALU.add).then_inc(taps_s, 1)
                dve.wait_ge(taps, n0 + 1)
                V.scalar_tensor_tensor(acc[0], u_p[:, j, 2:2 + TP], wj[2], acc[0], ALU.mult, ALU.add).then_inc(taps, 1)
                if last:
                    dve.wait_ge(taps_s, 2)
                    V.scalar_tensor_tensor(acc_s, u_s[:, j, 2:2 + NT, :], wj[2], acc_s, ALU.mult, ALU.add).then_inc(taps_s, 1)
                per = 4
                with dve.Fori(0, (CW - 3) // per) as i:
                    for k in range(3, 3 + per):
                        dve.wait_ge(taps, i * per + (n0 + k - 1))
                        V.scalar_tensor_tensor(acc[k % 2], u_p[:, j, bass.ds(i * per + k, TP)],
                                               wdT[:, bass.ds(i * (per * DC) + (k * DC + j), 1)], acc[k % 2],
                                               ALU.mult, ALU.add).then_inc(taps, 1)
                        if last:
                            dve.wait_ge(taps_s, i * per + k)
                            V.scalar_tensor_tensor(acc_s, u_s[:, j, bass.ds(i * per + k, NT), :],
                                                   wdT[:, bass.ds(i * (per * DC) + (k * DC + j), 1)], acc_s,
                                                   ALU.mult, ALU.add).then_inc(taps_s, 1)
                dve.wait_ge(taps, n0 + CW)
                V.tensor_tensor(acc[0], acc[0], acc[1], ALU.add).then_inc(taps, 1)

            dve.wait_ge(S("ln_mu"), 1)
            dve.wait_ge(S("convs"), 2 * CW * len(SMP_CONV))
            dve.wait_ge(taps, (CW + 1) * DC)
            dve.wait_ge(taps_s, CW)
            for cc in range(DC):
                V.tensor_tensor(y[:, cc, :], y[:, cc, :], mu[:], ALU.subtract).then_inc(S("ln_yc"), 1)
            dve.wait_ge(S("ln_rms"), 1)
            V.reciprocal(r[:], r[:]).then_inc(S("ln_r"), 1)
            dve.wait_ge(S("ln_r"), 1)
            dve.wait_ge(S("ln_yc"), DC)

            def ln_t(cc):
                if cc >= 2:
                    dve.wait_ge(S("ln_s"), cc - 1)
                V.tensor_tensor(t2[:, cc % 2, :], y[:, cc, :], r[:], ALU.mult).then_inc(S("ln_t"), 1)

            ln_t(0)
            ln_t(1)
            for cc in range(DC):
                if cc + 2 < DC:
                    ln_t(cc + 2)
                dve.wait_ge(S("ln_hi"), cc + 1)
                V.tensor_tensor(Hl[:, cc, :], y[:, cc, :], Hh[:, cc, :].bitcast(F32), ALU.subtract).then_inc(S("ln_lo"), 1)
            for m in range(DC):
                residual(0, m, U_PW2 + m)
                split_lo(U_PW2 + m + SPLIT_AHEAD)
                add_square(1, m)

            def ffn(layer):
                for hf in range(2):
                    u0 = U_FFN[layer] + hf * F_UNITS
                    q0 = (2 * layer + hf) * FHC
                    for p in range(FHC):
                        q = q0 + p
                        split_lo(u0 + 2 * p + SPLIT_AHEAD)
                        dve.wait_ge(tile_done, u0 + 2 * p + 2)
                        dve.wait_ge(S("ff_silu"), q + 1)
                        t = halves(t2[:, q % 2, :])
                        V.tensor_tensor(t, tile(u0 + 2 * p + 1), t, ALU.mult).then_inc(tile_free, 2)
                        split_lo(u0 + 2 * p + 1 + SPLIT_AHEAD)
                        dve.wait_ge(S("ff_hi"), q + 1)
                        V.tensor_tensor(al[:, p, :], t2[:, q % 2, :], ah[:, p, :].bitcast(F32), ALU.subtract).then_inc(S("ff_lo"), 1)
                    dve.wait_ge(x_upd, DC * (1 + 3 * layer + hf))
                    for m in range(DC):
                        u = u0 + 2 * FHC + m
                        residual(1 + 3 * layer + hf, m, u)
                        split_lo(u + SPLIT_AHEAD)
                        if hf:
                            add_square(2 + 2 * layer, m)

            dve.wait_ge(x_upd, 8)
            norm(1)
            ffn(0)
            dve.wait_ge(x_upd, 24)
            norm(2)
            dve.wait_ge(S("n_lo"), 27)

            def cmp_turn(b):
                dve.wait_ge(S("ct_pe"), b + 1)
                if b == 4:
                    dve.wait_ge(S("hs_pe"), 1)
                V.tensor_copy(CPk[:, b % 4].rearrange("p h q -> p (h q)"), ps[:, 6, :]).then_inc(S("cp_dve"), 1)

            def cmp_keys(g2):
                dve.wait_ge(S("kc_pe"), g2 + 1)
                src = ps[0:64, 6, 0:4 * NKV * NCS].rearrange("p (b h n) -> p h b n", b=4, h=NKV)
                for par in range(2):
                    V.tensor_copy(kcT_s[64 * par:64 * par + 64, :, 4 * g2:4 * g2 + 4, :], src[:, par::2]).then_inc(S("kc_dve"), 1)

            def cmp_pairs():
                dve.wait_ge(S("cr_out"), 16 * (1 + NT))
                for th in range(2 * NKV):
                    for par in range(2):
                        src = kvT[64 * (th % 2):64 * (th % 2) + 64, KV_SLOT[th // 2], par:TP:2]
                        V.tensor_copy(P2[64 * par:64 * par + 64, th, :], src).then_inc(S("p2"), 1)

            def cmp_prompt_out():
                dve.wait_ge(S("kc_pe"), 3)
                for par in range(2):
                    V.tensor_copy(kcT_p[64 * par:64 * par + 64, :, :],
                                  ps[0:64, 6, 0:G * NCP].rearrange("p (h n) -> p h n", n=NCP)[:, par::2, :]).then_inc(S("kc_dve"), 1)
                dve.wait_ge(S("kc_pe"), 4)
                V.tensor_copy(vc_p[0:NCP].rearrange("p h d -> p (h d)"), ps[0:NCP, 7, 0:NKV * HD]).then_inc(S("kc_dve"), 1)

            for f in range(12):
                u = U_KV + f
                dve.wait_ge(tile_done, u + 1)
                V.tensor_copy(halves(kvT[:, KV_SLOT[f], :]), tile(u)).then_inc(tile_free, 1)
                split_lo(u + SPLIT_AHEAD)
                if f == 9:
                    dve.wait_ge(tile_free, U_KV + 4)
                for what, arg in CMP_PLAN[f]:
                    if what == "turn":
                        cmp_turn(arg)
                    elif what == "keys":
                        cmp_keys(arg)
                    elif what == "pairs":
                        cmp_pairs()
                    elif what == "prompt_out":
                        cmp_prompt_out()
            dve.wait_ge(tile_free, U_IN)
            norm(3)
            for t in range(DC):
                u = U_IN + t
                dve.wait_ge(S("q_act"), 2 * (t + 1))
                kv = t // 2
                V.tensor_scalar(qs[64 * (kv % 2):64 * (kv % 2) + 64, kv // 2, :, 2 * (t % 2) + 1, :],
                                smp_cols(tile(u)[64:128]), -SCALE, None, ALU.mult).then_inc(S("q_dve"), 1)
                V.tensor_scalar(halves(qT[64 * (kv % 2):64 * (kv % 2) + 64, (kv // 2) * 4 + 2 * (t % 2) + 1, :]),
                                tile(u)[64:128], -SCALE, None, ALU.mult).then_inc(tile_free, 1)
                split_lo(u + SPLIT_AHEAD)
            u = U_IN + DC
            split_lo(u + SPLIT_AHEAD)
            dve.wait_ge(tile_done, u + 1)
            dve.wait_ge(tile_free, u)
            V.tensor_copy(halves(t2[0:3 * NH, 0, :]), tile(u, 3 * NH)).then_inc(tile_free, 1)
            dve.wait_ge(tile_free, u + 1)

            def scores(n):
                kv, i = n // 4, n % 4
                L = P * (i + 1)
                if i == 0:
                    if kv:
                        dve.wait_ge(S("sc"), 9 * n)
                    else:
                        dve.wait_ge(S("dist_in"), 16)
                    for g in range(G):
                        V.tensor_scalar(bias[:, g, :], dist[:], SLOPES[G * kv + g], None, ALU.mult).then_inc(S("bias"), 1)
                    dve.wait_ge(S("bias"), G * (kv + 1))
                if n >= 2:
                    dve.wait_ge(S("pt_pe"), pt0[n - 1])
                for s in range(8):
                    k = 9 * n + s
                    dve.wait_ge(S("sc_pe"), k + 1)
                    V.tensor_tensor_reduce(out=Pp[:, n % 2, s, 0:L], in0=ps[:, k % 4, 0:L], in1=bias[:, s // 2, TP - L:TP],
                                           scale=1.0, scalar=3.0e38, op0=ALU.add, op1=ALU.min,
                                           accum_out=nmin[:, n % 2, s:s + 1]).then_inc(S("sc"), 1)
                k = 9 * n + 8
                dve.wait_ge(S("sc_pe"), k + 1)
                z = Pc[:, n % 2]
                for g in range(G):
                    V.scalar_tensor_tensor(z[:, g, :], distc[:, i, :], SLOPES[G * kv + g], ps[:, k % 4, g * NCP:(g + 1) * NCP],
                                           ALU.mult, ALU.add).then_inc(S("zg") if g < 3 else S("sc"), 1)

            def shifted(n):
                z = Pc[:, n % 2]
                dve.wait_ge(S("zg"), 3 * (n + 1))
                dve.wait_ge(S("sc"), 9 * (n + 1))
                V.tensor_reduce(nmin[:, n % 2, 8:12], z, AX.X, ALU.min).then_inc(S("zc"), 1)
                dve.wait_ge(S("zc"), 2 * n + 1)
                V.tensor_tensor(z, z, nmin[:, n % 2, 8:12].unsqueeze(2).to_broadcast([P, G, NCP]), ALU.subtract).then_inc(S("zc"), 1)

            def weights(n):
                kv, i = n // 4, n % 4
                z, W = Pc[:, n % 2], S("wg")
                dve.wait_ge(S("pexp"), 9 * (n + 1))
                V.tensor_reduce(sums[:, n % 2, 8:12], z, AX.X, ALU.add).then_inc(W, 1)
                dve.wait_ge(W, 4 * n + 1)
                V.reciprocal(wgt[:, n % 2, :], sums[:, n % 2, :]).then_inc(W, 1)
                dve.wait_ge(W, 4 * n + 2)
                w8 = wgt[:, n % 2, 0:8].rearrange("p (g r) -> p g r", r=2)
                V.tensor_tensor(wgt[:, n % 2, 8:12], wgt[:, n % 2, 8:12], gates[:, i, G * kv:G * kv + G, 0], ALU.mult).then_inc(W, 1)
                V.tensor_tensor(w8, w8, gates[:, i, G * kv:G * kv + G, 1:3], ALU.mult).then_inc(S("pw"), 1)
                if i == 0:
                    V.tensor_tensor(z, z, maskc[:].unsqueeze(1).to_broadcast([P, G, NCP]), ALU.mult).then_inc(S("zmask"), 1)
                    dve.wait_ge(S("zmask"), kv + 1)
                dve.wait_ge(W, 4 * n + 3)
                V.tensor_tensor(z, z, wgt[:, n % 2, 8:12].unsqueeze(2).to_broadcast([P, G, NCP]), ALU.mult).then_inc(W, 1)

            def even_block(m, j):
                dve.wait_ge(S("pt_pe"), j + 1)
                if j >= 2:
                    dve.wait_ge(S("pv"), j - 1)
                K = NCP if j == pt0[m] else P
                V.tensor_copy(PT[0:K, 0, :], ps[0:K, 4, :]).then_inc(S("pt_dve"), 1)

            def result(m):
                if m % 2 == 0:
                    dve.wait_ge(S("pv"), pt0[m + 1])
                    kv, i = m // 4, m % 4
                    V.tensor_copy(oT[:, 2 * kv:2 * kv + 2, P * i:P * i + P],
                                  ps[:, 6, 0:2 * P].rearrange("p (g q) -> p g q", g=2)).then_inc(S("o_dve"), 1)

            def sample_gates():
                dve.wait_ge(S("gs_pe"), 2)
                dve.wait_ge(S("cb_in"), 16 * 5)
                dve.wait_ge(S("kc_dve"), 7)
                tm = t2[:, 1, 0:3 * TS].rearrange("p (f t) -> p f t", t=NT)
                V.tensor_tensor(tm, ps[:, 7, 0:3 * TS].rearrange("p (f t) -> p f t", t=NT),
                                tmask[:].unsqueeze(1).to_broadcast([P, 3 * NB, NT]), ALU.mult).then_inc(S("gs_dve"), 1)
                dve.wait_ge(S("gs_dve"), 1)
                V.reduce_sum(gs[:].rearrange("p a b -> p (a b)"), tm, AX.X).then_inc(S("gs_dve"), 1)

            for n in range(4 * NKV + 1):
                if n < 4 * NKV:
                    scores(n)
                if n == 0:
                    sample_gates()
                    dve.wait_ge(S("gates"), 1)
                if n >= 1:
                    even_block(n - 1, pt0[n - 1] + pt0[n - 1] % 2)
                if n < 4 * NKV:
                    shifted(n)
                if n >= 1:
                    for j in range(pt0[n - 1] + pt0[n - 1] % 2 + 2, pt0[n], 2):
                        even_block(n - 1, j)
                    result(n - 1)
                if n < 4 * NKV:
                    weights(n)

            dve.wait_ge(S("vc_pe"), 1)
            V.tensor_copy(vc_s[:].rearrange("p (a e) h d -> p a (e h d)", e=2), ps[0:NCS, 0:4, :]).then_inc(S("vc_dve"), 1)
            for b in range(NB + 1):
                if b < NB:
                    dve.wait_ge(S("kt_pe"), b + 1)
                    if b >= 1:
                        dve.wait_ge(S("s_sc"), b)
                    V.tensor_copy(KT[:, 0], ps[:, 4, :].rearrange("p (a e q) -> p a e q", a=2, e=2)).then_inc(S("kt_dve"), 1)
                if b >= 1:
                    m = b - 1
                    dve.wait_ge(S("s_pt"), m + 1)
                    if m:
                        dve.wait_ge(S("s_pv"), m)
                    V.tensor_copy(PTs[:, 0:2].rearrange("p a q -> p (a q)"), ps[:, 6, 0:256]).then_inc(S("s_ptd"), 1)
                    V.tensor_copy(PTs[0:TS, 2], ps[0:TS, 6, 256:384]).then_inc(S("s_ptd"), 1)
                    V.tensor_copy(PTs[0:NCS, 6], ps[0:NCS, 6, 384:512]).then_inc(S("s_ptd"), 1)
                if b < NB:
                    dve.wait_ge(S("s_sc"), b + 1)
                    if b == 0:
                        dve.wait_ge(S("tabs_in"), 16)
                    if b >= 2:
                        dve.wait_ge(S("s_pt"), b - 1)
                    bank, nm = 2 * (b % 2), nmin[:, b % 2, :]
                    for br in range(2):
                        V.tensor_tensor_reduce(out=Ps[:, b % 2, br, :], in0=ps[:, bank + br, 0:NKS], in1=tabs[:, b, :],
                                               scale=1.0, scalar=3.0e38, op0=ALU.add, op1=ALU.min,
                                               accum_out=nm[:, 1 + br:2 + br]).then_inc(S("s_z"), 1)
                    z = Pcs[:, b % 2, 0:NCS]
                    V.tensor_tensor(z, ps[:, bank, NKS:NKS + NCS], tabc[:], ALU.add).then_inc(S("s_z"), 1)
                    dve.wait_ge(S("s_z"), 5 * b + 3)
                    V.tensor_reduce(nm[:, 0:1], z, AX.X, ALU.min).then_inc(S("s_z"), 1)
                if b >= 1:
                    m = b - 1
                    dve.wait_ge(S("s_pv"), m + 1)
                    dst = oT[:, :, TP + NT * m:TP + NT * m + NT].rearrange("p (a k e) t -> p a k e t", a=2, k=2)
                    for kp in range(2):
                        src = ps[64 * kp:64 * kp + 64, 7, 384:448].rearrange("p (a e r t) -> p a e r t", a=2, e=2, r=2)
                        for par in range(2):
                            V.tensor_copy(dst[64 * par:64 * par + 64, :, kp], src[:, :, :, par]).then_inc(S("o_dve"), 1)
                if b < NB:
                    dve.wait_ge(S("s_exp"), 3 * (b + 1))
                    V.reciprocal(wgt[:, b % 2, 0:3], sums[:, b % 2, 0:3]).then_inc(S("s_z"), 1)
                    dve.wait_ge(S("s_z"), 5 * (b + 1))
                    V.tensor_tensor(wgt[:, b % 2, 0:3], wgt[:, b % 2, 0:3], gs[:, :, b], ALU.mult).then_inc(S("s_wgt"), 1)
                    dve.wait_ge(S("s_wgt"), b + 1)
                    z = Pcs[:, b % 2, 0:NCS]
                    V.tensor_scalar(z, z, wgt[:, b % 2, 0:1], None, ALU.mult).then_inc(S("s_pc"), 1)
            for cc in range(DC):
                dve.wait_ge(S("oh"), cc + 1)
                V.tensor_tensor(Hl[:, cc, :], oT[:, cc, :], Hh[:, cc, :].bitcast(F32), ALU.subtract).then_inc(S("ol"), 1)
            dve.wait_ge(x_upd, 24)
            for m in range(DC):
                residual(3, m, U_WO + m)
                split_lo(U_WO + m + SPLIT_AHEAD)
                add_square(3, m)
            dve.wait_ge(x_upd, 32)
            norm(4)
            ffn(1)
            dve.wait_ge(x_upd, 48)
            norm(5)
            for tb in range(5):
                n = P if tb < 4 else TS
                dve.wait_ge(S("f_pe"), tb + 1)
                if tb >= 2:
                    dve.wait_ge(S(f"y_out{tb % 2}"), 16 * (tb // 2))
                V.tensor_copy(stage[0:n, tb % 2, 0:512], ps[0:n, 2 * (tb % 3), :]).then_inc(S("fe_dve"), 1)

        @block.tensor
        def _(pe):
            M = nc.tensor.matmul

            def tr(out, in_):
                return nc.tensor.transpose(out, in_, ident[0:in_.shape[0], 0:in_.shape[0]])

            def dense(u, hi, lo, ready=None, tiles=1, midway=None):
                K, w = UNITS[u][2], UNITS[u][4]
                pe.wait_ge(lo_ready, u + tiles)
                if u + tiles > RING:
                    pe.wait_ge(tile_free, u + tiles - RING)
                for k in range(K):
                    if ready:
                        ready(k)
                    if midway and k == K // 2:
                        midway()
                    for v in range(u, u + tiles):
                        s = v % RING
                        for i, (wt, rt) in enumerate(((wh, hi), (wh, lo), (wl, hi))):
                            for h in range(2):
                                last = M(ps[0:w, 2 * s + h, 0:HT], wt[:, s, k, 0:w], rt[:, k, h * HT:(h + 1) * HT],
                                         start=(k == 0 and i == 0), stop=(k == K - 1 and i == 2))
                        if k == K - 1:
                            last.then_inc(tile_done, 1)

            def strip(s_):
                for hf in range(2):
                    n = 2 * s_ + hf
                    pe.wait_ge(ada_in[n % RING_ADA], 16 * (n // RING_ADA + 1))
                    if hf == 0 and s_:
                        pe.wait_ge(ada_row, s_)
                    for g in range(4):
                        last = M(ps[32 * g:32 * g + 32, 6, :], cpad[:, 4 * hf + g, :], ada[:, n % RING_ADA, g, :],
                                 start=(hf == 0), stop=(hf == 1))
                    last.then_inc(ada_used, 1)

            def turn_strip(s_):
                pe.wait_ge(ada_row, s_ + 1)
                if s_:
                    pe.wait_ge(ada_ev, 4 * s_)
                for k in range(4):
                    last = M(ps[:, 7, 16 * k:16 * k + 9], adarow[:, P * k:P * k + P], sel[:], start=True, stop=True)
                last.then_inc(ada_tr, 1)

            def sum_chunk(src, cc, done, n=DC):
                for h in range(2):
                    last = M(ps[:, 6 + h, 0:HT], ones[:], src[:, h * HT:(h + 1) * HT], start=(cc == 0), stop=(cc == n - 1))
                last.then_inc(done, 1)

            def stat(st):
                pe.wait_ge(S("st_add"), 6 * st)
                sum_chunk(mu, 0, S("st_ck"), 2)
                pe.wait_ge(S("st_sq"), DC * (st + 1))
                sum_chunk(t2[:, (DC - 1) % 2, :], 1, S("st_ck"), 2)

            def normed(k):
                def ready(cc):
                    pe.wait_ge(S("n_lo"), 9 * k + cc + 2)
                return ready

            pe.wait_ge(S("id_in"), 32)
            pe.wait_ge(S("vec_in"), 16 * 11)
            tr(ps[:, 7, 0:R_END], rows0[0:R_END, 0, :])
            tr(ps[:, 7, R_END:R_END + 124], rows0[0:124, 1, :])
            tr(ps[:, 7, R_END + 124:R_END + 248], rows0[0:124, 2, :])
            tr(ps[:, 7, 384:512], rows0[:, 3, :]).then_inc(S("vec_pe"), 1)
            pe.wait_ge(S("c_silu"), 1)
            tr(ps[:, 6, 0:72], rows0[0:72, 4, :]).then_inc(S("vec_pe"), 1)

            def block_in(bk):
                n = xi_rows[bk]
                pe.wait_ge(S(f"xi_in{bk % 2}"), 16 * (bk // 2 + 1))
                if bk >= 3:
                    pe.wait_ge(S("xi_dve"), bk - 2)
                    pe.wait_ge(S("xi_act"), bk - 2)
                for cc in range(DC):
                    last = tr(ps[:, 2 * (bk % 3) + cc // 4, (cc % 4) * n:(cc % 4 + 1) * n],
                              stage[0:n, bk % 2, cc * P:(cc + 1) * P])
                last.then_inc(S("xi_pe"), 1)

            for bk in range(5):
                block_in(bk)
                if bk in STRIP_BLOCKS:
                    s_ = STRIP_BLOCKS.index(bk)
                    if s_ == 0:
                        pe.wait_ge(S("const"), 4)
                        pe.wait_ge(S("vec_act"), 1)
                        pe.wait_ge(S("vec_dve"), 3)
                    strip(s_)
                    if s_:
                        turn_strip(s_ - 1)
            turn_strip(STRIPS_FIRST - 1)
            pe.wait_ge(ada_ev, 4 * STRIPS_FIRST)
            for cc in range(DC):
                if cc == 2:
                    block_in(5)
                    block_in(6)
                pe.wait_ge(S("st_sq"), cc + 1)
                sum_chunk(sqb[:, cc, :], cc, S("st_ck"))
            pe.wait_ge(S("st_rms"), 1)
            pe.wait_ge(S("xi_dve"), 7)
            pe.wait_ge(S("xi_act"), 7)
            dense(0, Hh, Hl, normed(0), tiles=RING)
            s_ = STRIPS_FIRST

            def next_strip():
                nonlocal s_
                strip(s_)
                if s_ > STRIPS_FIRST:
                    turn_strip(s_ - 1)
                s_ += 1

            for u in range(U_PW2):
                if u >= RING:
                    dense(u, Hh, Hl, midway=next_strip if STRIP_PLAN[u] > 1 else None)
                if STRIP_PLAN[u]:
                    next_strip()
            turn_strip(N_STRIP - 1)
            pe.wait_ge(tile_free, U_PW2)
            for cc in range(DC):
                tr(ps[0:CW - 1, cc // 4, (cc % 4) * P:(cc % 4 + 1) * P], u_p[:, cc, TP:TP + CW - 1])
            for cc in range(DC):
                last = tr(ps[0:TS, 2 + cc // 4, (cc % 4) * P:(cc % 4 + 1) * P],
                          u_s[:, cc, CW - 1:, :].rearrange("p t b -> p (t b)"))
            last.then_inc(S("cr_pe"), 1)
            pe.wait_ge(ada_ev, 16 * DC)
            for cc in range(DC):
                pe.wait_ge(S("convs"), 2 * CW * sum(c0 <= cc for c0, c1 in SMP_CONV))
                pe.wait_ge(S("conv"), (CW + 1) * (cc + 1))
                if cc == DC - 1:
                    pe.wait_ge(S("conv_s"), CW)
                sum_chunk(y[:, cc, :], cc, S("ln_pe"))
            pe.wait_ge(S("ln_mu"), 1)
            for cc in range(DC):
                pe.wait_ge(S("ln_sq"), cc + 1)
                sum_chunk(sqb[:, cc, :], cc, S("ln_pe"))

            def ln_ready(cc):
                pe.wait_ge(S("ln_lo"), cc + 1)

            pe.wait_ge(S("cr_ev"), 2)

            def updated(u0, K, hi, lo, st, ready, tiles):
                dense(u0, hi, lo, ready, tiles=tiles)
                for m in range(DC):
                    if m >= tiles:
                        dense(u0 + m, hi, lo)
                if st is not None:
                    stat(st)

            updated(U_PW2, DC, Hh, Hl, 1, ln_ready, RING)

            def ffn(layer, k):
                for hf in range(2):
                    u0 = U_FFN[layer] + hf * F_UNITS
                    q0 = (2 * layer + hf) * FHC
                    if hf == 0:
                        dense(u0, Hh, Hl, normed(k), tiles=RING)
                    for p in range(RING * (hf == 0), 2 * FHC):
                        dense(u0 + p, Hh, Hl)

                    def ready(cc):
                        pe.wait_ge(S("ff_lo"), q0 + cc + 1)

                    updated(u0 + 2 * FHC, FHC, ah, al, 2 + 2 * layer if hf else None, ready, 1)

            ffn(0, 1)

            w1s = (w1k, w1v)

            def cmp_bias():
                pe.wait_ge(S("w1_in"), 32)
                pe.wait_ge(S("st_rms"), 3)
                for t in range(2):
                    for j in range(LC // 2):
                        last = M(ps[:, 6, t:t + 1], w1s[t][:, j, :], vT[:, R_PE + 16 * t + j:R_PE + 16 * t + j + 1],
                                 start=(j == 0), stop=(j == LC // 2 - 1))
                last.then_inc(S("hp_pe"), 1)
                pe.wait_ge(S("hc"), 1)

            def cmp_turn(b):
                pe.wait_ge(S(f"cc_in{b % 2}"), 64 * (b // 2 + 1))
                if b:
                    pe.wait_ge(S("cp_dve"), b)
                    pe.wait_ge(S("cp_act"), b)
                if b == 4:
                    pe.wait_ge(S("kc_dve"), 2)
                    pe.wait_ge(S("hc"), 3)
                for t in range(2):
                    for h in range(NKV):
                        last = tr(ps[:, 6 + t, h * P:(h + 1) * P], Cb[b % 2][:, NKV * t + h].rearrange("p e d -> p (e d)"))
                last.then_inc(S("ct_pe"), 1)

            def cmp_hidden(g2):
                pe.wait_ge(S("cp_dve"), 4 * g2 + 4)
                pe.wait_ge(S("cp_act"), 4 * g2 + 4)
                n = 4 * NKV * NCS
                for t, cp in enumerate((CPk, CPv)):
                    for j in range(LC // 2):
                        last = M(ps[:, 6 + t, 0:n], w1s[t][:, j, :],
                                 cp[:].rearrange("p b h q -> p (b h) q")[:, :, j:j + 8 * (NCS - 1) + 1:8],
                                 start=(j == 0), stop=(j == LC // 2 - 1))
                    last.then_inc(S("hs_pe"), 1)

            def cmp_keys(g2):
                n = 4 * NKV * NCS
                pe.wait_ge(S("hc"), 2 + 2 * g2)
                M(ps[0:HD, 6, 0:n], w2t[:, 0, :], t2[:, 1, 0:n], start=True, stop=True).then_inc(S("kc_pe"), 1)

            def cmp_prompt():
                pe.wait_ge(S("p2"), 16)
                pe.wait_ge(S("kc_dve"), 4)
                pe.wait_ge(S("hc"), 5)
                for t in range(2):
                    for j in range(LC // 2):
                        last = M(ps[:, 6 + t, 0:G * NCP], w1s[t][:, j, :],
                                 P2[:, NKV * t:NKV * t + NKV, j:j + 8 * (NCP - 1) + 1:8],
                                 start=(j == 0), stop=(j == LC // 2 - 1))
                    last.then_inc(S("hp_pe"), 1)

            def cmp_prompt_out():
                pe.wait_ge(S("hc"), 7)
                M(ps[0:HD, 6, 0:G * NCP], w2t[:, 0, :], t2[:, 0, 0:G * NCP], start=True, stop=True).then_inc(S("kc_pe"), 1)
                for h in range(NKV):
                    last = M(ps[0:NCP, 7, h * HD:(h + 1) * HD], t2[:, 0, P + h * NCP:P + (h + 1) * NCP], w2t[:, 1, :],
                             start=True, stop=True)
                last.then_inc(S("kc_pe"), 1)

            pe.wait_ge(S("cb_in"), 16 * 5)
            dense(U_KV, Hh, Hl, normed(2), tiles=RING)
            for f in range(12):
                if f >= RING:
                    dense(U_KV + f, Hh, Hl)
                for what, arg in CMP_PLAN[f]:
                    if what == "bias":
                        cmp_bias()
                    elif what == "turn":
                        cmp_turn(arg)
                    elif what == "hidden":
                        cmp_hidden(arg)
                    elif what == "keys":
                        cmp_keys(arg)
                    elif what == "prompt":
                        cmp_prompt()
                    elif what == "prompt_out":
                        cmp_prompt_out()

            def rows(k):
                tb, g3 = k // 3, k % 3
                n = P if tb < 4 else TS
                if k >= 2:
                    pe.wait_ge(S("rt_ev"), 5 * ((k - 2) // 3) + (1, 3, 5)[(k - 2) % 3])
                for ff in range(4):
                    last = tr(ps[0:n, 6 + k % 2, ff * P:(ff + 1) * P], kvT[:, KV_SLOT[4 * g3 + ff], tb * P:tb * P + n])
                last.then_inc(S("rt_pe"), 1)

            pe.wait_ge(S("kc_dve"), 7)
            dense(U_IN, Hh, Hl, normed(3), tiles=RING)
            for t in range(DC + 1):
                if t >= RING:
                    dense(U_IN + t, Hh, Hl)
                for k in RT_PLAN.get(t, []):
                    rows(k)
            def turn_gates():
                pe.wait_ge(S("q_act"), 2 * DC + 1)
                pe.wait_ge(S("rt_ev"), 25)
                for i in range(4):
                    last = tr(ps[:, 6, 48 * i:48 * i + 48], t2[0:3 * NH, 0, P * i:P * i + P])
                last.then_inc(S("gs_pe"), 1)
                pe.wait_ge(S("expd_in"), 16)
                for br in range(3):
                    last = M(ps[:, 7, TS * br:TS * br + TS], expd[:, br, :], t2[0:3 * NH, 0, TP:T], start=True, stop=True)
                last.then_inc(S("gs_pe"), 1)
                pe.wait_ge(S("gates"), 1)
                pe.wait_ge(S("gs_dve"), 1)

            def scores(n):
                kv, i = n // 4, n % 4
                L, b64 = P * (i + 1), 64 * (kv % 2)

                def free(k):
                    if k >= 4:
                        pe.wait_ge(S("sc"), k - 3)

                for s in range(8):
                    k = 9 * n + s
                    free(k)
                    M(ps[:, k % 4, 0:L], qT[b64:b64 + 64, (kv // 2) * 4 + s // 2, P * i:P * i + P],
                      kvT[b64:b64 + 64, 2 * (s % 2) + kv // 2, 0:L], start=True, stop=True).then_inc(S("sc_pe"), 1)
                k = 9 * n + 8
                free(k)
                for g in range(G):
                    last = M(ps[:, k % 4, g * NCP:(g + 1) * NCP], qT[b64:b64 + 64, (kv // 2) * 4 + g, P * i:P * i + P],
                             kcT_p[b64:b64 + 64, kv // 2, :], start=True, stop=True)
                last.then_inc(S("sc_pe"), 1)

            def values(n):
                kv, i = n // 4, n % 4
                steps = [(2, 0)] + [(br, kb) for br in range(2) for kb in range(i + 1)]
                pe.wait_ge(S("wg"), 4 * (n + 1))
                if n >= 2:
                    pe.wait_ge(S("o_act") if n % 2 else S("o_dve"), n // 2)

                def turn(x_):
                    j, (br, kb) = pt0[n] + x_, steps[x_]
                    if br < 2 and kb == 0:
                        pe.wait_ge(S("scaled"), 8 * n + 4 * (br + 1))
                    if j >= 2:
                        pe.wait_ge(S("pt_act") if j % 2 else S("pt_dve"), j // 2)
                    for g in range(G):
                        src = Pp[:, n % 2, 2 * g + br, kb * P:(kb + 1) * P] if br < 2 else Pc[:, n % 2, g, :]
                        K = P if br < 2 else NCP
                        last = tr(ps[0:K, 4 + j % 2, g * P:(g + 1) * P], src)
                    last.then_inc(S("pt_pe"), 1)

                def product(x_):
                    j, (br, kb) = pt0[n] + x_, steps[x_]
                    pe.wait_ge(S("pt_act") if j % 2 else S("pt_dve"), j // 2 + 1)
                    v = vrow[:, kb, br, kv, :] if br < 2 else vc_p[0:NCP, kv, :]
                    K = P if br < 2 else NCP
                    for par in range(2):
                        last = M(ps[64 * par:64 * par + 64, 6 + n % 2, 0:2 * P], v,
                                 PT[0:K, j % 2, :].rearrange("p (g q) -> p g q", g=G)[:, par::2, :],
                                 start=(x_ == 0), stop=(x_ == len(steps) - 1))
                    last.then_inc(S("pv"), 1)

                for x_ in range(len(steps)):
                    turn(x_)
                    if x_:
                        product(x_ - 1)
                product(len(steps) - 1)

            pe.wait_ge(tile_free, U_WO)
            pe.wait_ge(S("q_act"), 2 * DC)
            pe.wait_ge(S("rt_ev"), 25)
            for n in range(4 * NKV + 1):
                if n < 4 * NKV:
                    scores(n)
                if n:
                    values(n - 1)
                else:
                    turn_gates()

            pe.wait_ge(S("sc"), 9 * 4 * NKV)
            for b in range(NB):
                for h in range(NKV):
                    q = NCS * (NKV * b + h)
                    last = M(ps[0:NCS, b // 2, (b % 2) * 256 + HD * h:(b % 2) * 256 + HD * h + HD],
                             hv_s[:, q:q + NCS], w2t[:, 1, :], start=True, stop=True)
            last.then_inc(S("vc_pe"), 1)
            pe.wait_ge(S("pt_dve"), pt0[-1] - pt0[-1] // 2)
            pe.wait_ge(S("pt_act"), pt0[-1] // 2)
            pe.wait_ge(S("vc_dve"), 1)
            pe.wait_ge(S("o_dve"), 8)
            pe.wait_ge(S("o_act"), 8)
            for b in range(NB + 1):
                if b < NB:
                    pe.wait_ge(S(f"s_in{b % 4}"), 48 * (b // 4 + 1))
                    if b:
                        pe.wait_ge(S("kt_dve"), b)
                        pe.wait_ge(S("kt_act"), b)
                    for bank, rows_ in ((4, Cs), (5, Cw)):
                        for kp in range(2):
                            for par in range(2):
                                q = (2 * kp + par) * P
                                last = tr(ps[:, bank, q:q + P], rows_[b % 4][:, par, kp * P:(kp + 1) * P])
                    last.then_inc(S("kt_pe"), 1)
                if b >= 1:
                    m = b - 1
                    pe.wait_ge(S("s_scaled"), 2 * (m + 1))
                    pe.wait_ge(S("s_pc"), m + 1)
                    if m:
                        pe.wait_ge(S("s_ptd"), 3 * m)
                        pe.wait_ge(S("s_pta"), 2 * m)
                        pe.wait_ge(S("o_dve"), 8 + 4 * m)
                    for br in range(2):
                        for kb in range(3):
                            K = P if kb < 2 else TS
                            tr(ps[0:K, 6 + br, kb * P:(kb + 1) * P], Ps[:, m % 2, br, kb * P:kb * P + K])
                    tr(ps[0:NCS, 6, 384:512], Pcs[:, m % 2, 0:NCS]).then_inc(S("s_pt"), 1)
                if b < NB:
                    pe.wait_ge(S("kt_dve"), b + 1)
                    pe.wait_ge(S("kt_act"), b + 1)
                    if b >= 2:
                        pe.wait_ge(S("s_z"), 5 * (b - 1))
                    bank = 2 * (b % 2)
                    for kv in range(NKV):
                        b64, o32 = 64 * (kv % 2), 32 * kv
                        q = qs[b64:b64 + 64, kv // 2, b].rearrange("p g t -> p (g t)")
                        for br in range(2):
                            M(ps[o32:o32 + 32, bank + br, 0:PAST], q, KT[b64:b64 + 64, br, kv // 2].rearrange("p e q -> p (e q)"),
                              start=True, stop=True)
                            last = M(ps[o32:o32 + 32, bank + br, PAST:NKS], q, kvT[b64:b64 + 64, 2 * br + kv // 2, TP:T],
                                     start=True, stop=True)
                        last = M(ps[o32:o32 + 32, bank, NKS:NKS + NCS], q, kcT_s[b64:b64 + 64, kv // 2, b, :],
                                 start=True, stop=True)
                    last.then_inc(S("s_sc"), 1)
                if b >= 1:
                    pe.wait_ge(S("s_ptd"), 3 * (m + 1))
                    pe.wait_ge(S("s_pta"), 2 * (m + 1))
                    lists = []
                    for kv in range(NKV):
                        cols = slice(32 * kv, 32 * kv + 32)
                        parts = []
                        for br, rows_ in ((0, Cs), (1, Cw)):
                            for par in range(2):
                                parts.append((rows_[m % 4][:, par, 256 + 64 * kv:320 + 64 * kv], PTs[:, 3 * br + par, cols]))
                            parts.append((vrow[0:TS, 4, br, kv, :], PTs[0:TS, 3 * br + 2, cols]))
                        parts.append((vc_s[:, m, kv, :], PTs[0:NCS, 6, cols]))
                        lists.append(parts)
                    for a_ in range(2):
                        c0 = 384 + 32 * a_
                        for x_ in range(7):
                            for e_ in range(2):
                                lhs, rhs = lists[2 * a_ + e_][x_]
                                last = M(ps[64 * e_:64 * e_ + HD, 7, c0:c0 + 32], lhs, rhs,
                                         start=(x_ == 0), stop=(x_ == 6))
                    last.then_inc(S("s_pv"), 1)

            def o_ready(cc):
                pe.wait_ge(S("ol"), cc + 1)

            pe.wait_ge(S("o_dve"), 8 + 4 * NB)
            updated(U_WO, DC, Hh, Hl, 3, o_ready, RING)
            ffn(1, 4)
            def turn_final(tb, cc):
                n = P if tb < 4 else TS
                return tr(ps[0:n, 2 * (tb % 3) + cc // 4, (cc % 4) * P:(cc % 4 + 1) * P], xf[:, cc, tb * P:tb * P + n])

            for cc in range(DC):
                pe.wait_ge(S("n_hi"), 9 * 5 + cc + 1)
                for tb in range(3):
                    last = turn_final(tb, cc)
                    if cc == DC - 1:
                        last.then_inc(S("f_pe"), 1)
            pe.wait_ge(S("n_s"), 18)
            for tb in (3, 4):
                pe.wait_ge(S("fe_act"), tb - 2)
                pe.wait_ge(S("fe_dve"), tb - 2)
                for cc in range(DC):
                    last = turn_final(tb, cc)
                last.then_inc(S("f_pe"), 1)


_OUTS = [("y_prompt", (1, 512, 1024)), ("y_sample", (8, 8, 1024)), ("kv_prompt", (4, 128, 4, 4, 64)),
         ("kv_sample", (8, 8, 4, 4, 64)), ("win_prompt", (1, 512, 2, 4, 64)), ("win_sample", (8, 264, 2, 4, 64)),
         ("conv_prompt", (1, 1, 30, 1024)), ("conv_sample", (1, 8, 30, 1024))]


def shape_constants():
    import numpy as np

    f = np.float32
    q = np.arange(P)[:, None]
    d = q + (TP - P) - np.arange(TP)[None, :]
    dist = np.where(d >= 0, d, FAR)
    i = np.arange(4)[None, :, None]
    dc = P * i + q[:, :, None] - (ST * np.arange(NCP)[None, None, :] + LC - 1)
    distc = np.where(dc >= 0, dc, FAR)
    row_h, row_t = np.arange(P) // NT, np.arange(P) % NT
    sl = np.array(SLOPES)[row_h][:, None]
    pos = np.concatenate([2 * np.arange(P), 2 * np.arange(P) + 1])
    tabs = np.zeros((P, NB, NKS))
    tabs[:, :, :PAST] = (sl * (PAST + row_t[:, None] - pos[None, :]))[:, None, :]
    dn = row_t[:, None] - np.arange(NT)[None, :]
    tabs[:, :, PAST:] = FAR
    for b in range(NB):
        tabs[:, b, PAST + NT * b:PAST + NT * b + NT] = np.where(dn >= 0, sl * dn, FAR)
    tabc = sl * (PAST + row_t[:, None] - (ST * np.arange(NCS)[None, :] + LC - 1))
    expd = np.zeros((3 * NH, 3, P))
    for h in range(NH):
        for br in range(3):
            expd[3 * h + br, br, NT * h:NT * h + NT] = 1
    sel = np.zeros((P, 1 + NB))
    for g in range(4):
        sel[32 * g + np.arange(1 + NB), np.arange(1 + NB)] = 1
    return {"ident": np.eye(P).astype(f), "sel": sel.astype(f), "dist": dist.astype(f), "distc": distc.astype(f),
            "maskc": (dc[:, 0, :] >= 0).astype(f), "tmask": (row_t[:, None] == np.arange(NT)[None, :]).astype(f),
            "tabs": tabs.astype(f), "tabc": tabc.astype(f), "expd": expd.astype(f)}


def kernel(**inputs):
    import numpy as _np
    import concourse.bacc as _bacc
    from concourse import mybir as _mybir
    from concourse.bass_utils import run_bass_kernel_spmd as _run

    nc = _bacc.Bacc("TRN2", target_bir_lowering=False, num_devices=1)
    arrays, a, o, c = {}, {}, {}, {}
    for group, named in ((a, inputs), (c, shape_constants())):
        for name, v in named.items():
            v = _np.ascontiguousarray(v)
            key = f"in_{name}_dram"
            arrays[key] = v
            group[name] = nc.dram_tensor(key, v.shape, _mybir.dt.from_np(v.dtype), kind="ExternalInput").ap()
    for name, shape in _OUTS:
        o[name] = nc.dram_tensor(f"out_{name}_dram", shape, F32, kind="ExternalOutput").ap()
    build(nc, a, o, c)
    res = _run(nc, [arrays], core_ids=[0])
    return tuple(res.results[0][f"out_{name}_dram"] for name, _ in _OUTS)
```
